# Optimizing a Trainium2 kernel written in Bass

```python
import math
import jax
import jax.numpy as jnp
from jax import lax
import numpy as np

D_MODEL = 1024
BATCH = 1
SEQ = 1024
DEPTH = 1
DEC_BATCH = 8
DEC_SEQ = 4
PAST_LEN = 4096
PAGE_SIZE = 128

LRU_WIDTH = 768
LRU_BLOCKS = 12
LRU_BLOCK = LRU_WIDTH // LRU_BLOCKS
CONV_W = 4
RG_C = 8.0
SSM_WIDTH = 512
SSM_GROUP = 16
SSM_GROUPS = SSM_WIDTH // SSM_GROUP
SSM_STATE = 64
ATTN_HEADS = 12
HEAD_DIM = 64
ATTN_WIDTH = ATTN_HEADS * HEAD_DIM
DILATED_GROUPS = ((128, 1), (512, 4), (2048, 16))
W_MAX = max(w for w, _ in DILATED_GROUPS)
Q_BLOCK = 128
N_BRANCH = 3
D_FF = 4 * D_MODEL
IN_COLS = LRU_WIDTH + SSM_WIDTH + 3 * ATTN_WIDTH + N_BRANCH * D_MODEL
SPLITS = (LRU_WIDTH, LRU_WIDTH + SSM_WIDTH, LRU_WIDTH + SSM_WIDTH + ATTN_WIDTH,
          LRU_WIDTH + SSM_WIDTH + 2 * ATTN_WIDTH, LRU_WIDTH + SSM_WIDTH + 3 * ATTN_WIDTH)
RMS_EPS = 1e-6
NEG_INF = -1e30

kernel_name = 'hybrid_rglru_s5_dilated_attn_decode_step'

def rms_norm(x, g):
    xf = x.astype(jnp.float32)
    y = xf * lax.rsqrt(jnp.mean(xf * xf, axis=-1, keepdims=True) + RMS_EPS)
    return (y * g.astype(jnp.float32)).astype(x.dtype)

def _linear_combine(e1, e2):
    a1, b1 = e1
    a2, b2 = e2
    return a1 * a2, a2 * b1 + b2

def _complex_combine(e1, e2):
    ar1, ai1, br1, bi1 = e1
    ar2, ai2, br2, bi2 = e2
    return (ar1 * ar2 - ai1 * ai2, ar1 * ai2 + ai1 * ar2,
            ar2 * br1 - ai2 * bi1 + br2, ar2 * bi1 + ai2 * br1 + bi2)

def rglru_branch(xa, conv_state, h0, conv_w, conv_b, wr, br, wi, bi, lam):
    B, T, _ = xa.shape
    xe = jnp.concatenate([conv_state.astype(xa.dtype), xa], axis=1)
    xc = conv_b.astype(jnp.float32) + sum(conv_w[i].astype(jnp.float32) * xe[:, i:i + T].astype(jnp.float32)
                                          for i in range(CONV_W))
    new_conv = xe[:, T:]
    xb = xc.reshape(B, T, LRU_BLOCKS, LRU_BLOCK)
    r = jax.nn.sigmoid(jnp.einsum('btnc,ncd->btnd', xb, wr.astype(jnp.float32)) + br).reshape(B, T, LRU_WIDTH)
    i_g = jax.nn.sigmoid(jnp.einsum('btnc,ncd->btnd', xb, wi.astype(jnp.float32)) + bi).reshape(B, T, LRU_WIDTH)
    log_a = -RG_C * jax.nn.softplus(-lam.astype(jnp.float32)) * r
    a = jnp.exp(log_a)
    mult = jnp.sqrt(jnp.maximum(-jnp.expm1(2.0 * log_a), 0.0))
    b = mult * (i_g * xc)
    b = b.at[:, 0].add(a[:, 0] * h0.astype(jnp.float32))
    _, h = lax.associative_scan(_linear_combine, (a, b), axis=1)
    return h.astype(xa.dtype), new_conv, h[:, -1]

def s5_branch(u, s0_re, s0_im, lam_re, lam_im, log_dt, b_re, b_im, c_re, c_im, d_skip, glu_w, glu_b):
    B, T, _ = u.shape
    ug = u.astype(jnp.float32).reshape(B, T, SSM_GROUPS, SSM_GROUP)
    lr = lam_re.astype(jnp.float32)
    li = lam_im.astype(jnp.float32)
    dt = jnp.exp(log_dt.astype(jnp.float32))[:, None]
    mag = jnp.exp(lr * dt)
    ang = li * dt
    ab_re = mag * jnp.cos(ang)
    ab_im = mag * jnp.sin(ang)
    den = lr * lr + li * li
    f_re = ((ab_re - 1.0) * lr + ab_im * li) / den
    f_im = (ab_im * lr - (ab_re - 1.0) * li) / den
    br_ = b_re.astype(jnp.float32)
    bi_ = b_im.astype(jnp.float32)
    bb_re = f_re[..., None] * br_ - f_im[..., None] * bi_
    bb_im = f_re[..., None] * bi_ + f_im[..., None] * br_
    bu_re = jnp.einsum('btgc,gnc->btgn', ug, bb_re)
    bu_im = jnp.einsum('btgc,gnc->btgn', ug, bb_im)
    s0r = s0_re.astype(jnp.float32)
    s0i = s0_im.astype(jnp.float32)
    bu_re = bu_re.at[:, 0].add(ab_re * s0r - ab_im * s0i)
    bu_im = bu_im.at[:, 0].add(ab_re * s0i + ab_im * s0r)
    a_re = jnp.broadcast_to(ab_re, (1, T) + ab_re.shape)
    a_im = jnp.broadcast_to(ab_im, (1, T) + ab_im.shape)
    _, _, s_re, s_im = lax.associative_scan(_complex_combine, (a_re, a_im, bu_re, bu_im), axis=1)
    y = (jnp.einsum('btgn,gcn->btgc', s_re, c_re.astype(jnp.float32))
         - jnp.einsum('btgn,gcn->btgc', s_im, c_im.astype(jnp.float32))
         + d_skip.astype(jnp.float32) * ug)
    z = jax.nn.gelu(y.reshape(B, T, SSM_WIDTH))
    gl = z @ glu_w.astype(jnp.float32) + glu_b.astype(jnp.float32)
    out = gl[..., :SSM_WIDTH] * jax.nn.sigmoid(gl[..., SSM_WIDTH:])
    return out.astype(u.dtype), s_re[:, -1], s_im[:, -1]

def _from_sub(a, T):
    B, d, nb, qb = a.shape[:4]
    rest = a.shape[4:]
    a = a.reshape((B, d, nb * qb) + rest)
    a = jnp.moveaxis(a, 1, 2)
    return a.reshape((B, nb * qb * d) + rest)[:, :T]

def dilated_window_attention(q, k_new, v_new, k_past, v_past):
    B, T, H, Dh = q.shape
    P = k_past.shape[1]
    front = jnp.zeros((B, W_MAX - P, H, Dh), q.dtype)
    k_all = jnp.concatenate([front, k_past.astype(q.dtype), k_new], axis=1)
    v_all = jnp.concatenate([front, v_past.astype(q.dtype), v_new], axis=1)
    scale = HEAD_DIM ** -0.5
    outs, maxes, dens = [], [], []
    for w, d in DILATED_GROUPS:
        n_back = w // d
        n_q = -(-T // d)
        qb = min(Q_BLOCK, n_q)
        n_blk = -(-n_q // qb)
        n_q_pad = n_blk * qb
        t_pad = n_q_pad * d - T
        qg = jnp.pad(q, ((0, 0), (0, t_pad), (0, 0), (0, 0))).reshape(B, n_q_pad, d, H, Dh)
        qg = jnp.moveaxis(qg, 2, 1).reshape(B, d, n_blk, qb, H, Dh)

        def to_sub(a):
            a = jnp.pad(a[:, W_MAX - w:], ((0, 0), (0, t_pad), (0, 0), (0, 0)))
            a = a.reshape(B, n_back + n_q_pad, d, H, Dh)
            return jnp.moveaxis(a, 2, 1)

        idx = jnp.arange(n_blk)[:, None] * qb + jnp.arange(qb + n_back)[None, :]
        kb = to_sub(k_all)[:, :, idx]
        vb = to_sub(v_all)[:, :, idx]
        s = jnp.einsum('brnqhc,brnkhc->brnhqk', qg, kb, preferred_element_type=jnp.float32) * scale
        qq = jnp.arange(qb)[:, None]
        kk = jnp.arange(qb + n_back)[None, :]
        band = (kk >= qq) & (kk <= qq + n_back)
        res = jnp.arange(d)[:, None, None]
        key_ok = idx[None] * d + res >= w - min(w, P)
        mask = band[None, None, None] & key_ok[:, :, None, None, :]
        s = jnp.where(mask[None], s, NEG_INF)
        m = jnp.max(s, axis=-1, keepdims=True)
        p = jnp.exp(s - m)
        den = jnp.sum(p, axis=-1)
        den_t = jnp.moveaxis(den, -1, -2)
        o = jnp.einsum('brnhqk,brnkhc->brnqhc', p, vb.astype(jnp.float32)) / den_t[..., None]
        outs.append(_from_sub(o, T))
        maxes.append(_from_sub(jnp.moveaxis(m[..., 0], -1, -2), T))
        dens.append(_from_sub(den_t, T))
    m_all = jnp.stack(maxes, axis=0)
    m_top = jnp.max(m_all, axis=0, keepdims=True)
    alpha = jnp.stack(dens, axis=0) * jnp.exp(m_all - m_top)
    o_all = jnp.stack(outs, axis=0)
    out = jnp.sum(alpha[..., None] * o_all, axis=0) / jnp.sum(alpha, axis=0)[..., None]
    return out.astype(q.dtype)

def decoder_layer(x, conv_state, lru_state, ssm_re, ssm_im, k_past, v_past, lp):
    B, T, _ = x.shape
    h = rms_norm(x, lp['norm_pre_mix'])
    proj = h @ lp['w_in']
    xa, u, q, k, v, gates = jnp.split(proj, SPLITS, axis=-1)
    q = q.reshape(B, T, ATTN_HEADS, HEAD_DIM)
    k = k.reshape(B, T, ATTN_HEADS, HEAD_DIM)
    v = v.reshape(B, T, ATTN_HEADS, HEAD_DIM)
    ya, new_conv, new_lru = rglru_branch(xa, conv_state, lru_state, lp['conv_w'], lp['conv_b'],
                                         lp['lru_wr'], lp['lru_br'], lp['lru_wi'], lp['lru_bi'], lp['lru_lambda'])
    yb, new_re, new_im = s5_branch(u, ssm_re, ssm_im, lp['ssm_lambda_re'], lp['ssm_lambda_im'], lp['ssm_log_dt'],
                                   lp['ssm_b_re'], lp['ssm_b_im'], lp['ssm_c_re'], lp['ssm_c_im'], lp['ssm_d'],
                                   lp['glu_w'], lp['glu_b'])
    yc = dilated_window_attention(q, k, v, k_past, v_past).reshape(B, T, ATTN_WIDTH)
    g = jax.nn.sigmoid(gates.astype(jnp.float32)).reshape(B, T, N_BRANCH, D_MODEL)
    merged = (g[:, :, 0] * (ya @ lp['w_proj_a']).astype(jnp.float32)
              + g[:, :, 1] * (yb @ lp['w_proj_b']).astype(jnp.float32)
              + g[:, :, 2] * (yc @ lp['w_proj_c']).astype(jnp.float32))
    x = x + rms_norm(merged.astype(x.dtype) @ lp['w_out'], lp['norm_post_mix'])
    h2 = rms_norm(x, lp['norm_pre_mlp'])
    ff = jnp.square(jax.nn.relu(h2 @ lp['mlp_w1'])) @ lp['mlp_w2']
    x = x + rms_norm(ff, lp['norm_post_mlp'])
    return x, new_conv, new_lru, new_re, new_im, k, v

def setup_inputs(seed: int = 0) -> dict:
    key = jax.random.key(seed)
    ks = jax.random.split(key, 40)
    f32 = jnp.float32

    def nrm(k, shape, scale):
        return jax.random.normal(k, shape, f32) * scale

    w_buf = min(W_MAX, PAST_LEN)
    u_lru = jax.random.uniform(ks[20], (DEPTH, LRU_WIDTH), f32, 0.9, 0.999)
    p_lru = u_lru ** (1.0 / RG_C)
    lru_lambda = jnp.log(p_lru) - jnp.log1p(-p_lru)
    lam_im_base = math.pi * jnp.arange(SSM_STATE, dtype=f32)
    return {
        'x_prompt': nrm(ks[0], (BATCH, SEQ, D_MODEL), 1.0),
        'x_sample': nrm(ks[1], (DEC_BATCH, DEC_SEQ, D_MODEL), 1.0),
        'state_conv': nrm(ks[2], (DEPTH, DEC_BATCH, CONV_W - 1, LRU_WIDTH), 1.0),
        'state_lru': nrm(ks[3], (DEPTH, DEC_BATCH, LRU_WIDTH), 0.5),
        'state_ssm_re': nrm(ks[4], (DEPTH, DEC_BATCH, SSM_GROUPS, SSM_STATE), 0.1),
        'state_ssm_im': nrm(ks[5], (DEPTH, DEC_BATCH, SSM_GROUPS, SSM_STATE), 0.1),
        'cache_k': nrm(ks[6], (DEPTH, DEC_BATCH, w_buf, ATTN_HEADS, HEAD_DIM), 1.0),
        'cache_v': nrm(ks[7], (DEPTH, DEC_BATCH, w_buf, ATTN_HEADS, HEAD_DIM), 1.0),
        'norm_pre_mix': 1.0 + nrm(ks[8], (DEPTH, D_MODEL), 0.02),
        'norm_post_mix': 1.0 + nrm(ks[9], (DEPTH, D_MODEL), 0.02),
        'norm_pre_mlp': 1.0 + nrm(ks[10], (DEPTH, D_MODEL), 0.02),
        'norm_post_mlp': 1.0 + nrm(ks[11], (DEPTH, D_MODEL), 0.02),
        'w_in': nrm(ks[12], (DEPTH, D_MODEL, IN_COLS), D_MODEL ** -0.5),
        'conv_w': nrm(ks[13], (DEPTH, CONV_W, LRU_WIDTH), CONV_W ** -0.5),
        'conv_b': nrm(ks[14], (DEPTH, LRU_WIDTH), 0.01),
        'lru_wr': nrm(ks[15], (DEPTH, LRU_BLOCKS, LRU_BLOCK, LRU_BLOCK), LRU_BLOCK ** -0.5),
        'lru_br': nrm(ks[16], (DEPTH, LRU_BLOCKS, LRU_BLOCK), 0.01),
        'lru_wi': nrm(ks[17], (DEPTH, LRU_BLOCKS, LRU_BLOCK, LRU_BLOCK), LRU_BLOCK ** -0.5),
        'lru_bi': nrm(ks[18], (DEPTH, LRU_BLOCKS, LRU_BLOCK), 0.01),
        'lru_lambda': lru_lambda,
        'ssm_lambda_re': -0.5 + nrm(ks[21], (DEPTH, SSM_GROUPS, SSM_STATE), 0.01),
        'ssm_lambda_im': lam_im_base + nrm(ks[22], (DEPTH, SSM_GROUPS, SSM_STATE), 0.01),
        'ssm_log_dt': jax.random.uniform(ks[23], (DEPTH, SSM_GROUPS), f32, math.log(0.001), math.log(0.1)),
        'ssm_b_re': nrm(ks[24], (DEPTH, SSM_GROUPS, SSM_STATE, SSM_GROUP), (2 * SSM_GROUP) ** -0.5),
        'ssm_b_im': nrm(ks[25], (DEPTH, SSM_GROUPS, SSM_STATE, SSM_GROUP), (2 * SSM_GROUP) ** -0.5),
        'ssm_c_re': nrm(ks[26], (DEPTH, SSM_GROUPS, SSM_GROUP, SSM_STATE), (2 * SSM_STATE) ** -0.5),
        'ssm_c_im': nrm(ks[27], (DEPTH, SSM_GROUPS, SSM_GROUP, SSM_STATE), (2 * SSM_STATE) ** -0.5),
        'ssm_d': nrm(ks[28], (DEPTH, SSM_GROUPS, SSM_GROUP), 1.0),
        'glu_w': nrm(ks[29], (DEPTH, SSM_WIDTH, 2 * SSM_WIDTH), SSM_WIDTH ** -0.5),
        'glu_b': nrm(ks[30], (DEPTH, 2 * SSM_WIDTH), 0.01),
        'w_proj_a': nrm(ks[31], (DEPTH, LRU_WIDTH, D_MODEL), LRU_WIDTH ** -0.5),
        'w_proj_b': nrm(ks[32], (DEPTH, SSM_WIDTH, D_MODEL), SSM_WIDTH ** -0.5),
        'w_proj_c': nrm(ks[33], (DEPTH, ATTN_WIDTH, D_MODEL), ATTN_WIDTH ** -0.5),
        'w_out': nrm(ks[34], (DEPTH, D_MODEL, D_MODEL), D_MODEL ** -0.5),
        'mlp_w1': nrm(ks[35], (DEPTH, D_MODEL, D_FF), D_MODEL ** -0.5),
        'mlp_w2': nrm(ks[36], (DEPTH, D_FF, D_MODEL), D_FF ** -0.5),
    }

def reference(x_prompt, x_sample, state_conv, state_lru, state_ssm_re, state_ssm_im, cache_k, cache_v,
              norm_pre_mix, norm_post_mix, norm_pre_mlp, norm_post_mlp, w_in, conv_w, conv_b,
              lru_wr, lru_br, lru_wi, lru_bi, lru_lambda, ssm_lambda_re, ssm_lambda_im, ssm_log_dt,
              ssm_b_re, ssm_b_im, ssm_c_re, ssm_c_im, ssm_d, glu_w, glu_b,
              w_proj_a, w_proj_b, w_proj_c, w_out, mlp_w1, mlp_w2):
    Bp, Tp, _ = x_prompt.shape
    keep = min(W_MAX, Tp)
    xp = x_prompt
    xs = x_sample
    p_conv, p_lru, p_re, p_im, p_k, p_v = [], [], [], [], [], []
    s_conv, s_lru, s_re, s_im, s_k, s_v = [], [], [], [], [], []
    for l in range(DEPTH):
        lp = {
            'norm_pre_mix': norm_pre_mix[l], 'norm_post_mix': norm_post_mix[l],
            'norm_pre_mlp': norm_pre_mlp[l], 'norm_post_mlp': norm_post_mlp[l],
            'w_in': w_in[l], 'conv_w': conv_w[l], 'conv_b': conv_b[l],
            'lru_wr': lru_wr[l], 'lru_br': lru_br[l], 'lru_wi': lru_wi[l], 'lru_bi': lru_bi[l],
            'lru_lambda': lru_lambda[l],
            'ssm_lambda_re': ssm_lambda_re[l], 'ssm_lambda_im': ssm_lambda_im[l], 'ssm_log_dt': ssm_log_dt[l],
            'ssm_b_re': ssm_b_re[l], 'ssm_b_im': ssm_b_im[l], 'ssm_c_re': ssm_c_re[l], 'ssm_c_im': ssm_c_im[l],
            'ssm_d': ssm_d[l], 'glu_w': glu_w[l], 'glu_b': glu_b[l],
            'w_proj_a': w_proj_a[l], 'w_proj_b': w_proj_b[l], 'w_proj_c': w_proj_c[l], 'w_out': w_out[l],
            'mlp_w1': mlp_w1[l], 'mlp_w2': mlp_w2[l],
        }
        zc = jnp.zeros((Bp, CONV_W - 1, LRU_WIDTH), xp.dtype)
        zl = jnp.zeros((Bp, LRU_WIDTH), jnp.float32)
        zs = jnp.zeros((Bp, SSM_GROUPS, SSM_STATE), jnp.float32)
        zk = jnp.zeros((Bp, 0, ATTN_HEADS, HEAD_DIM), xp.dtype)
        xp, c_, h_, r_, i_, k_, v_ = decoder_layer(xp, zc, zl, zs, zs, zk, zk, lp)
        p_conv.append(c_); p_lru.append(h_); p_re.append(r_); p_im.append(i_)
        p_k.append(k_[:, Tp - keep:]); p_v.append(v_[:, Tp - keep:])
        xs, c_, h_, r_, i_, k_, v_ = decoder_layer(xs, state_conv[l], state_lru[l], state_ssm_re[l],
                                                   state_ssm_im[l], cache_k[l], cache_v[l], lp)
        s_conv.append(c_); s_lru.append(h_); s_re.append(r_); s_im.append(i_)
        s_k.append(k_); s_v.append(v_)
    return (xp, xs,
            jnp.stack(p_conv), jnp.stack(p_lru), jnp.stack(p_re), jnp.stack(p_im), jnp.stack(p_k), jnp.stack(p_v),
            jnp.stack(s_conv), jnp.stack(s_lru), jnp.stack(s_re), jnp.stack(s_im), jnp.stack(s_k), jnp.stack(s_v))


_drawn_inputs = setup_inputs


def setup_inputs(seed=0):
    import zlib

    import numpy as np

    out = dict(_drawn_inputs(seed))
    spreads = {}
    factors = {'norm_pre_mix': 2.932,
     'norm_post_mix': 3.8,
     'norm_pre_mlp': 13.931,
     'norm_post_mlp': 17.749,
     'lru_br': 32.686,
     'lru_bi': 25.24,
     'ssm_lambda_re': 14.29,
     'glu_b': 8.0,
     'conv_b': 2.708,
     'ssm_c_re': 3.096,
     'ssm_c_im': 3.199}
    for name, (base, spread) in spreads.items():
        noise = np.random.default_rng([zlib.crc32(name.encode()), seed]).standard_normal(out[name].shape)
        drawn = base * np.exp(spread * noise) if base else spread * noise
        out[name] = jnp.asarray(drawn.astype(out[name].dtype))
    for name, factor in factors.items():
        out[name] = (out[name] * factor).astype(out[name].dtype)
    return out
```

```python
from contextlib import ExitStack

import numpy as np

import concourse.bass as bass
from concourse import mybir

F32 = mybir.dt.float32
F32R = mybir.dt.float32r
ALU = mybir.AluOpType
ACT = mybir.ActivationFunctionType

P = 128
D = 1024
KD = D // P
T = 1024
NB, TS = 8, 4
NS = NB * TS
N = T + NS
NBLK, BLK = 3, (T + NS) // 3
LRU, S5W, AW, DFF = 768, 512, 768, 4096
HEADS, HD = 12, 64
HP = HEADS // 2
CW = 4
G, GC, NST = 32, 16, 64
J = G // 2
L = 8
C = T // L
EPS = 1e-6
W_MAX = 2048
GROUPS = ((128, 1), (512, 4), (2048, 16))
NEAR = 512
NCK = NEAR + (W_MAX - NEAR) // 16 * TS
KT = NCK // P
NK = NCK + NS
HQ = HEADS * TS
MASKED = -1e30
TINY = 2.0 ** -100
SCALE = HD ** -0.5

T_U, T_XA, T_Q, T_K, T_V = S5W // P, LRU // P, HP, HP, HP
T_GATE = 3 * KD
T_IN = T_U + T_XA + T_Q + T_K + T_V + T_GATE
K_B = S5W // P
K_A = K_C = LRU // P
FCH = 4
NCH = DFF // P // FCH
SINGLE, DOUBLE = 1, 2
PAIRS = ([SINGLE] * (T_IN // 2) + [DOUBLE] * 2 + [DOUBLE] * 2 + [SINGLE] * 4 + [SINGLE] * 4 + [SINGLE] * 4
         + [SINGLE] * 2 + [SINGLE, SINGLE, DOUBLE, DOUBLE] * (NCH - 1) + [DOUBLE] * 2)
P_GLU = T_IN // 2
P_B = P_GLU + 2
P_A = P_B + 2
P_C = P_A + 4
P_OUT = P_C + 4
P_MLP = P_OUT + 4
USES = [sum(PAIRS[:i]) for i in range(len(PAIRS) + 1)]
R_XA, R_Q, R_K, R_V = 0, T_XA, T_XA + T_Q, T_XA + T_Q + T_K
T_KEEP = T_XA + T_Q + T_K + T_V
TWO_PI_HI = 6.28125
TWO_PI_MID = float(np.float32(np.floor((2 * np.pi - TWO_PI_HI) * 2 ** 20) / 2 ** 20))
TWO_PI_LO = float(2 * np.pi - TWO_PI_HI - TWO_PI_MID)
ROUND = 1.5 * 2.0 ** 23


UNITS = 4 * KD
V_GRAN, P_GRAN, GRAN = {}, {}, 0
for _x in range(-1, UNITS + 1):
    if (_x + 1) % (2 * KD) == 0 and _x + 1 < UNITS:
        V_GRAN[_x + 1] = [GRAN, GRAN + 1]
        GRAN += 2
    if 0 <= _x < UNITS:
        P_GRAN[_x] = [GRAN + _k for _k in range((_x % KD) // 4 + 1)]
        GRAN += len(P_GRAN[_x])


def transposed(u):
    return P_GRAN[u][-1] + 1 if u >= 0 else P_GRAN[u + UNITS][-1] + 1 - GRAN


def wait(eng, sem, value):
    if isinstance(value, int) and value <= 0:
        return
    eng.wait_ge(sem, value)


class Steps:

    def __init__(self, eng, sem):
        self.eng, self.sem, self.n, self.base = eng, sem, 0, 0

    def __call__(self, ins):
        ins.then_inc(self.sem, 1)
        self.n += 1
        self.eng.wait_ge(self.sem, self.n + self.base)

    def repeat(self, count, body):
        n0 = self.n
        body(0)
        per = self.n - n0
        if count > 1:
            with self.eng.Fori(1, count) as i:
                self.base = (i - 1) * per if per else 0
                body(i)
                assert self.n - n0 == 2 * per
            self.base = 0
        self.n = n0 + count * per


def hybrid_layer(nc, t):
    v, s, pe = nc.vector, nc.scalar, nc.tensor
    with ExitStack() as ctx:
        def sem(name):
            return ctx.enter_context(nc.semaphore(name))

        def sems(name, n):
            return [sem(f"{name}{i}") for i in range(n)]

        def own(name, shape, dt=F32):
            return ctx.enter_context(nc.sbuf_tensor(name, shape, dt))

        w_raw = own("w_raw", [P, 2, KD * P])
        w_hi = own("w_hi", [P, 2, KD, P], F32R)
        w_lo = own("w_lo", [P, 2, KD, P], F32R)
        zeros = own("zeros", [P, KD * P])
        stage = own("stage", [P, 2, N])
        ident = own("ident", [P, P])
        ones = own("ones", [P, P])
        gains = own("gains", [P, 4, KD])
        glu_b = own("glu_b", [P, 2, K_B])
        lam = own("lam", [P, T_XA])
        lru_k = own("lru_k", [P, T_XA])
        sp = own("sp", [P, 5, T_XA])
        ROW = 4 * N
        AREA = 2 * KD * ROW
        arena = own("arena", [P, (2 * AREA + AREA // 2) // 4])
        base = nc.sbuf_base - (2 * AREA + AREA // 2)
        areas = {"A": (base, AREA), "B": (base + AREA, AREA), "R": (base + 2 * AREA, AREA // 2)}

        def at(area, off, name, shape, dt=F32):
            start, size = areas[area]
            assert off + 4 * int(np.prod(shape[1:])) <= size, name
            return nc.alloc_sbuf_tensor_at(name, shape, dt, offset=start + off)

        op_hi = at("A", 0, "op_hi", [P, KD, N], F32R)
        op_lo = at("A", AREA // 2, "op_lo", [P, KD, N], F32R)
        hid_hi = at("B", 0, "hid_hi", [P, 2 * FCH, N], F32R)
        hid_lo = at("B", AREA // 2, "hid_lo", [P, 2 * FCH, N], F32R)
        acc = at("R", 0, "acc", [P, KD, N])
        resid = at("B", 0, "resid", [P, KD, N])
        n_sq = at("B", AREA // 2, "n_sq", [P, 2, N])
        n_sum = at("B", AREA // 2 + 2 * ROW, "n_sum", [P, N])
        n_rs = at("B", AREA // 2 + 3 * ROW, "n_rs", [P, N])
        n_rstd = at("B", AREA // 2 + 4 * ROW, "n_rstd", [P, N])
        n_tmp = at("B", AREA // 2 + 5 * ROW, "n_tmp", [P, 2, N])
        gate_t = at("B", 6 * ROW, "gate_t", [P, 2, N])
        prod_t = at("B", AREA // 2 + 6 * ROW, "prod_t", [P, 2, N])

        rx = at("B", 0, "rx", [P, 2, J, L + 1, GC])
        wt = at("B", 18432, "wt", [P, 2, J, L, GC])
        z5 = at("B", 18432, "z5", [P, 2, J, C])
        ph = at("B", 34816, "ph", [P, 2, J, C])
        t5 = at("B", 51200, "t5", [P, 2, J * C])
        dec = at("R", 0, "dec", [P, J, C])
        st = at("R", 8192, "st", [P, 2, J, C + 1])
        pw = at("R", 24704, "pw", [P, 2, J, L + 1])
        pwr = at("R", 25856, "pwr", [P, 2, J, L])
        bb = at("R", 26880, "bb", [P, 2, J, GC])
        bc_in = at("R", 28928, "bc_in", [P, 2, 2, J, GC])
        s5_in = at("R", 33024, "s5_in", [P, 3, J])
        s5_d = at("R", 33216, "s5_d", [GC, G])
        s5_t = own("s5_t", [P, 24, J])
        p_fin = own("p_fin", [P, 2, J])
        wtt = at("A", 0, "wtt", [P, 2, J, P])
        toep = at("A", 16384, "toep", [P, G, P])
        kpad = at("A", 32768, "kpad", [GC, G, 7 * GC + P])
        ug = at("A", 32768, "ug", [P, G, C])
        yg = at("A", 49152, "yg", [P, G, C])
        flat = stage[:, :, :].rearrange("p b n -> p (b n)")
        us = flat[:, 0:512].rearrange("p (a g b) -> p a g b", a=2, g=G)
        ys = flat[:, 512:768].rearrange("p (g b) -> p g b", g=G)
        s0 = flat[:, 768:1024].rearrange("p (a j b) -> p a j b", a=2, j=J)
        sf = flat[:, 1024:1280].rearrange("p (a j b) -> p a j b", a=2, j=J)
        sq = flat[:, 1280:1792].rearrange("p (a j b) -> p a j b", a=4, j=J)

        lru = []
        for n, area in enumerate("AB"):
            def r(k, area=area, n=n, shape=None):
                return at(area, k * ROW, f"lru{k}_{n}", shape or [P, N])
            lru.append(dict(xc=r(0), r=r(1), i=r(2), t=r(3), q=r(4), a=r(5), u=r(6), m=r(7), b=r(8), h=r(9),
                            x=r(10, shape=[P, CW - 1 + T]), xs=at(area, 12 * ROW, f"lru_xs{n}", [P, NB, CW - 1 + TS]),
                            w=at(area, 12 * ROW + 256, f"lru_w{n}", [P, 2, P]),
                            par=at(area, 12 * ROW + 1280, f"lru_par{n}", [P, 16]),
                            k=at(area, 12 * ROW + 1344, f"lru_k{n}", [P, 1]),
                            h0=at(area, 12 * ROW + 1376, f"lru_t{n}", [P, NB])))

        qkv = at("A", 0, "qkv", [P, 2, 3, T])
        vn = at("A", 24576, "vn", [P, 2, KD, P])
        bias = at("A", 32768, "bias", [P, T])
        sm = at("A", 36864, "sm", [P, 2, T])
        pm = at("A", 45056, "pm", [P, 2, T])
        pt = at("A", 53248, "pt", [P, 2, KD, P])
        mx = at("A", 61440, "mx", [P, 2, 4])
        yo = at("R", 0, "yo", [P, 2, T])

        kc = [at(a, 0, f"kc{n}", [P, HP, NCK]) for n, a in enumerate("BA")]
        vc = [at(a, 21504, f"vc{n}", [P, KT, AW]) for n, a in enumerate("BA")]
        sqd = at("B", 43008, "sqd", [P, HP, NB, HQ])
        sq1 = at("B", 52224, "sq1", [P, 2, HP, HQ])
        qkvs = at("B", 54528, "qkvs", [P, 3, HP, NS])
        vnew = at("B", 56832, "vnew", [NS, HP, P])
        pts = at("B", 59904, "pts", [P, 2, KT + 1, HQ])
        yos = at("B", 62976, "yos", [P, HP, NB, TS])
        sbias = at("A", 43008, "sbias", [HQ, 2, NK])
        sms = at("A", 50432, "sms", [HQ, 2, NK])
        pms = at("R", 8192, "pms", [HQ, 2, NK])
        mxs = at("R", 16384, "mxs", [HQ, 2, 4])

        ps = ctx.enter_context(nc.psum_tensor("ps", [P, 8, 512], F32))

        def blocks(ap):
            return ap.rearrange("p (b n) -> p b n", b=NBLK)

        def pset(b):
            return ps[:, 3 * b:3 * b + 3, 0:BLK]

        w_loaded = sems("w_loaded", 2)
        w_split = sems("w_split", 2)
        w_zero, w_half = sem("w_zero"), sem("w_half")
        mm_ready = sems("mm_ready", 2)
        mm_free = sems("mm_free", 2)
        act_own, dve_own = sem("act_own"), sem("dve_own")
        stored = sems("stored", 2)
        const_in, x_in, s5_par_in = sem("const_in"), sem("x_in"), sem("s5_par_in")

        class NormSems:
            def __init__(self, name):
                self.sq = sem(name + "_sq")
                self.added = sem(name + "_added")
                self.sum = sem(name + "_sum")
                self.rs = sem(name + "_rs")
                self.h = sem(name + "_h")
                self.hi = sem(name + "_hi")
                self.lo = sem(name + "_lo")

        n_in, n_mix, n_pre, n_ff = (NormSems(x) for x in ("n_in", "n_mix", "n_pre", "n_ff"))
        a5, d5, d5p = sem("a5"), sem("d5"), sem("d5p")
        p5 = sem("p5")
        toep_in, ug_in, us_in, yd_out, st_out = (sem(x) for x in ("toep_in", "ug_in", "us_in", "yd_out", "st_out"))
        s0_in = sem("s0_in")
        lru_in = sems("lru_in", 2)
        lru_stored = sems("lru_stored", 2)
        lru_xc, lru_mm, lru_sig, lru_u, lru_sq, lru_h = (
            sem("lru_" + x) for x in ("xc", "mm", "sig", "u", "sq", "h"))
        lam_e, lam_a = sem("lam_e"), sem("lam_a")
        at_in = sems("at_in", 2)
        bias_in = sem("bias_in")
        at_s, at_masked, at_nb, at_p, at_pn, at_t, at_pt, at_pv, at_o = (
            sem("at_" + x) for x in ("s", "masked", "nb", "p", "pn", "t", "pt", "pv", "o"))
        yo_out = sems("yo_out", 2)
        qkvs_in = sem("qkvs_in")
        kv_in = sems("kv_in", 2)
        sa_q, sa_vt, sa_vn, sa_q1, sa_s, sa_masked, sa_nb, sa_p, sa_pn, sa_t, sa_pt, sa_pv, sa_o = (
            sem("sa_" + x) for x in ("q", "vt", "vn", "q1", "s", "masked", "nb", "p", "pn", "t", "pt", "pv", "o"))
        yos_out = sem("yos_out")
        op_in = sems("op_in", 2)
        g_act, op_h, op_l = sem("g_act"), sem("op_h"), sem("op_l")
        glu_y = sem("glu_y")
        glu_h, glu_l = sem("glu_h"), sem("glu_l")
        gate_in = sems("gate_in", 2)
        merged = sem("merged")
        o_hi, o_lo = sem("o_hi"), sem("o_lo")
        x_again, x2_done, x2_out, x2_in, y_done, y_out = (
            sem(x) for x in ("x_again", "x2_done", "x2_out", "x2_in", "y_done", "y_out"))
        go = sem("go")
        sq_done, hid_h, hid_l = sem("sq_done"), sem("hid_h"), sem("hid_l")

        block = ctx.enter_context(nc.Block())

        @block.sync
        def _(sy):
            def weights(i):
                for b in range(2):
                    wait(sy, w_split[b], i)
                    src = t["w"].rearrange("(i b) p k -> i b p k", b=2)
                    src = src[i, b] if isinstance(i, int) else src[bass.ds(i, 1), b].rearrange("a p k -> p (a k)")
                    sy.dma_start(w_raw[:, b], src).then_inc(w_loaded[b], 16)

            def weight_pairs(first, last):
                with sy.Fori(first, last) as i:
                    weights(i)

            for k in range(KD):
                sy.dma_start(acc[:, k], t["x"][:, k]).then_inc(x_in, 16)
            sy.dma_start(ident[:], t["ident"]).then_inc(const_in, 16)
            sy.dma_start(ones[:], t["ones"]).then_inc(const_in, 16)
            sy.dma_start(gains[:], t["gains"]).then_inc(const_in, 16)
            sy.dma_start(glu_b[:], t["glu_b"]).then_inc(const_in, 16)
            sy.dma_start(lam[:], t["lam"]).then_inc(const_in, 16)
            weights(0)
            sy.wait_ge(n_in.h, KD)
            sy.dma_start(s5_in[:], t["s5_par"]).then_inc(s5_par_in, 16)
            sy.dma_start(bc_in[:], t["s5_bc"]).then_inc(s5_par_in, 16)
            sy.dma_start(s5_d[:], t["s5_d"]).then_inc(s5_par_in, 16)
            weight_pairs(1, P_GLU + 1)

            sy.wait_ge(d5, 3)
            for tau in range(L):
                off = (L - 1 - tau) * GC
                sy.dma_start(toep[tau * GC:(tau + 1) * GC], kpad[:, :, off:off + P]).then_inc(toep_in, 16)
            for b in range(2):
                sy.wait_ge(stored[b], 16 * (T_IN // 2))
            sy.wait_ge(d5, 4)
            sy.dma_start(s0, t["s0"]).then_inc(s0_in, 16)
            u_d = t["u_d"].rearrange("(g c) n -> c g n", c=GC)
            for a in range(2):
                for tau in range(TS):
                    row = (a * TS + tau) * GC
                    sy.dma_start(us[row:row + GC, a], u_d[:, :, T + tau * NB:T + (tau + 1) * NB]).then_inc(us_in, 16)
            sy.wait_ge(toep_in, 16 * L)
            for tau in range(L):
                sy.dma_start(ug[tau * GC:(tau + 1) * GC], u_d[:, :, tau * C:(tau + 1) * C]).then_inc(ug_in, 16)
            sy.wait_ge(d5, 8)
            sy.dma_start(t["p_ssm"], p_fin[:]).then_inc(st_out, 16)
            sy.dma_start(t["s_ssm"], sf).then_inc(st_out, 16)
            sy.wait_ge(d5, 9)
            sy.wait_ge(a5, 7)
            y_d = t["y5_d"].rearrange("(g c) n -> c g n", c=GC)
            for tau in range(L):
                rows = slice(tau * GC, (tau + 1) * GC)
                sy.dma_start(y_d[:, :, tau * C:(tau + 1) * C], yg[rows]).then_inc(yd_out, 16)
                if tau < TS:
                    sy.dma_start(y_d[:, :, T + tau * NB:T + (tau + 1) * NB], ys[rows]).then_inc(yd_out, 16)
            sy.wait_ge(yd_out, 16 * (L + TS))
            sy.wait_ge(st_out, 32)

            def lru_load(i):
                for b in range(2):
                    def pick(x, i=i, b=b):
                        x = x.rearrange("(i b) p k -> i b p k", b=2)
                        return x[i, b] if isinstance(i, int) else x[bass.ds(i, 1), b].rearrange("a p k -> p (a k)")
                    z = lru[b]
                    wait(sy, lru_stored[b], 16 * i)
                    xa = pick(t["keep"][R_XA:R_XA + T_XA])
                    sy.dma_start(z["x"][:, CW - 1:], xa[:, 0:T]).then_inc(lru_in[b], 16)
                    sy.dma_start(z["xs"][:, :, CW - 1:], xa[:, T:N].rearrange("p (b t) -> p b t", b=NB)).then_inc(lru_in[b], 16)
                    sy.dma_start(z["xs"][:, :, 0:CW - 1], pick(t["conv_s"]).rearrange("p (b t) -> p b t", b=NB)).then_inc(lru_in[b], 16)
                    sy.dma_start(z["w"][:].rearrange("p a m -> p (a m)"), pick(t["lru_w"])).then_inc(lru_in[b], 16)
                    sy.dma_start(z["par"][:], pick(t["lru_par"])).then_inc(lru_in[b], 16)

            def lru_store(i):
                for b in range(2):
                    out = t["ya"].rearrange("(i b) p k -> i b p k", b=2)
                    out = out[i, b] if isinstance(i, int) else out[bass.ds(i, 1), b].rearrange("a p k -> p (a k)")
                    wait(sy, lru_h, 2 * i + b + 1)
                    sy.dma_start(out, lru[b]["h"][:]).then_inc(lru_stored[b], 16)

            lru_load(0)
            lru_store(0)
            with sy.Fori(1, T_XA // 2) as i:
                lru_load(i)
                lru_store(i)
            for b in range(2):
                sy.wait_ge(lru_stored[b], 16 * (T_XA // 2))

            def kept(row, i, b):
                x = t["keep"][row:row + HP].rearrange("(i b) p k -> i b p k", b=2)
                return x[i, b] if isinstance(i, int) else x[bass.ds(i, 1), b].rearrange("a p k -> p (a k)")

            def at_load(i):
                for b in range(2):
                    wait(sy, at_pv, 32 * i + 16 * b - 16)
                    for n, row in enumerate((R_Q, R_K, R_V)):
                        sy.dma_start(qkv[:, b, n], kept(row, i, b)[:, 0:T]).then_inc(at_in[b], 16)

            def at_store(i):
                for b in range(2):
                    out = t["yc"].rearrange("(i b) p k -> i b p k", b=2)
                    out = out[i, b] if isinstance(i, int) else out[bass.ds(i, 1), b].rearrange("a p k -> p (a k)")
                    wait(sy, at_o, 8 * i + 4 * b + 4)
                    sy.sem_inc(go, 1)
                    sy.dma_start(out[:, 0:T], yo[:, b]).then_inc(yo_out[b], 16)

            sy.dma_start(bias[:], t["bias"]).then_inc(bias_in, 16)
            at_load(0)
            for n, row in enumerate((R_Q, R_K, R_V)):
                sy.dma_start(qkvs[:, n], t["keep"][row:row + HP, :, T:N].rearrange("h p n -> p h n")).then_inc(qkvs_in, 16)

            def kv_load(i):
                for b in range(2):
                    def pick(x, i=i, b=b):
                        x = x.rearrange("(i b) p k -> i b p k", b=2)
                        return x[i, b] if isinstance(i, int) else x[bass.ds(i, 1), b].rearrange("a p k -> p (a k)")
                    wait(sy, sa_pv, 2 * i + b - 1)
                    sy.dma_start(kc[b][:].rearrange("p h n -> p (h n)"), pick(t["k_cache"])).then_inc(kv_in[b], 16)
                    sy.dma_start(vc[b][:].rearrange("p h n -> p (h n)"), pick(t["v_cache"])).then_inc(kv_in[b], 16)
                    sy.dma_start(sbias[:, b], pick(t["sbias"])).then_inc(kv_in[b], 16)

            at_store(0)
            with sy.Fori(1, HP // 2) as i:
                at_load(i)
                at_store(i)
            for b in range(2):
                sy.wait_ge(yo_out[b], 16 * (HP // 2))
            kv_load(0)
            with sy.Fori(1, NB // 2) as i:
                kv_load(i)
            sy.wait_ge(sa_o, NB)
            sy.dma_start(t["yc"][:, :, T:N].rearrange("h p n -> p h n"), yos[:].rearrange("p h b t -> p h (b t)")).then_inc(yos_out, 16)
            sy.wait_ge(yos_out, 16)

            ops = [t["y5_d"].rearrange("(k p) n -> k p n", p=P)[k] for k in range(K_B)]
            for n in range(K_B):
                wait(sy, op_l, n - 1)
                sy.dma_start(stage[:, n % 2], ops[n]).then_inc(op_in[n % 2], 16)
            weights(P_GLU + 1)
            gates = t["gate_d"].rearrange("(j i b) p k -> j i b p k", j=3, b=2)

            def gate_load(branch, i, tile0):
                for b in range(2):
                    g = gates[branch]
                    g = g[i, b] if isinstance(i, int) else g[bass.ds(i, 1), b].rearrange("a p k -> p (a k)")
                    wait(sy, merged, tile0 + 2 * i + b - 1)
                    sy.dma_start(gate_t[:, b], g).then_inc(gate_in[b], 16)

            def operand_load(first, src, k):
                wait(sy, op_l, first + k - 1)
                sy.dma_start(stage[:, k % 2], src[k]).then_inc(op_in[k % 2], 16)

            gate_load(1, 0, 0)
            weights(P_B)
            for k in range(K_A):
                operand_load(K_B, t["ya"], k)
            weights(P_B + 1)
            for m in range(1, KD // 2):
                gate_load(1, m, 0)
            weights(P_A)
            gate_load(0, 0, KD)
            for k in range(K_C):
                operand_load(K_B + K_A, t["yc"], k)
            with sy.Fori(1, KD // 2) as i:
                weights(i + P_A)
                gate_load(0, i, KD)
            weights(P_C)
            gate_load(2, 0, 2 * KD)
            with sy.Fori(1, KD // 2) as i:
                weights(i + P_C)
                gate_load(2, i, 2 * KD)
            sy.wait_ge(merged, 3 * KD)
            for k in range(KD):
                sy.dma_start(resid[:, k], t["x"][:, k]).then_inc(x_again, 16)
            weight_pairs(P_OUT, P_MLP + 1)
            for k in range(KD):
                sy.wait_ge(x2_done, k + 1)
                sy.dma_start(t["x2_d"][:, k], resid[:, k]).then_inc(x2_out, 16)
            weight_pairs(P_MLP + 1, len(PAIRS))
            sy.wait_ge(x2_out, 16 * KD)
            sy.wait_ge(mm_ready[1], USES[-1])
            sy.wait_ge(mm_ready[0], USES[-1])
            for k in range(KD):
                sy.dma_start(resid[:, k], t["x2_d"][:, k]).then_inc(x2_in, 16)
            for k in range(KD):
                sy.wait_ge(y_done, k + 1)
                sy.dma_start(t["y"][:, k], resid[:, k]).then_inc(y_out, 16)
            sy.wait_ge(y_out, 16 * KD)

        @block.gpsimd
        def _(pool):
            pool.memset(zeros[:], 0.0).then_inc(w_zero, 1)
            pool.wait_ge(w_zero, 1)

            def split(i, b, used):
                if used:
                    pool.wait_ge(mm_ready[used[0]], used[1])
                pool.wait_ge(w_loaded[b], 16 * (i + 1))
                hi, lo = (w[:, b].rearrange("p k m -> p (k m)") for w in (w_hi, w_lo))
                pool.tensor_tensor(hi, w_raw[:, b], zeros[:], ALU.add).then_inc(w_half, 1)
                pool.wait_ge(w_half, 2 * i + b + 1)
                pool.tensor_tensor(lo, w_raw[:, b], hi.bitcast(F32), ALU.subtract).then_inc(w_split[b], 1)

            def pair(i, before, uses):
                for b in range(2):
                    split(i, b, (b, uses + 1) if before == SINGLE else (1, uses + 1 + b))

            def run(first, last):
                kind, u0 = PAIRS[first - 1], USES[first - 1]
                assert all(k == kind for k in PAIRS[first - 1:last - 1])
                if last - first == 1:
                    pair(first, kind, u0)
                else:
                    with pool.Fori(first, last) as i:
                        pair(i, kind, (i - first) * kind + u0)

            for b in range(2):
                split(0, b, None)
            run(1, P_GLU + 1)
            run(P_GLU + 1, P_A + 1)
            run(P_A + 1, P_MLP + 3)
            first, per = P_MLP + 3, USES[P_MLP + 6] - USES[P_MLP + 2]
            with pool.Fori(0, NCH - 1) as c:
                for n in range(4):
                    pair(c * 4 + first + n, PAIRS[first + n - 1], c * per + USES[first + n - 1])
            run(len(PAIRS) - 1, len(PAIRS))

        @block.scalar
        def _(act):
            step = Steps(act, act_own)

            def squares(n, src, ready):
                for k in range(KD):
                    ready(k)
                    wait(act, n.added, k - 1)
                    s.activation(n_sq[:, k % 2], src[:, k], ACT.Square).then_inc(n.sq, 1)

            def root(n):
                act.wait_ge(n.sum, 1)
                s.activation(blocks(n_rs[:]), pset(0), ACT.Sqrt, bias=EPS, scale=1.0 / D).then_inc(n.rs, 1)

            def high_parts(n):
                for k in range(KD):
                    act.wait_ge(n.h, k + 1)
                    s.activation(op_hi[:, k], n_tmp[:, k % 2], ACT.Copy).then_inc(n.hi, 1)

            act.wait_ge(lam_a, 1)
            s.activation(sp[:, 1], sp[:, 0], ACT.Exp, scale=-1.0).then_inc(lam_e, 1)
            squares(n_in, acc, lambda k: act.wait_ge(x_in, 16 * KD))
            root(n_in)
            high_parts(n_in)
            act.wait_ge(s5_par_in, 48)
            s.activation(s5_t[:, 0], s5_in[:, 2], ACT.Tanh, scale=1.0 / 16).then_inc(a5, 1)
            act.wait_ge(d5p, 1)
            s.activation(s5_t[:, 4], s5_t[:, 2], ACT.Tanh, scale=0.5).then_inc(a5, 1)
            s.activation(s5_t[:, 5], s5_t[:, 3], ACT.Sin).then_inc(a5, 1)
            s.activation(s5_t[:, 6], s5_t[:, 3], ACT.Sin, scale=0.5).then_inc(a5, 1)

            def stage_free(i, b):
                act.wait_ge(mm_ready[b], i + 1)
                wait(act, stored[b], 16 * i)

            def store(i, b, dst):
                act.wait_ge(mm_free[b], i + 1)
                act.dma_start(dst, stage[:, b]).then_inc(stored[b], 16)

            for i in range(T_U // 2):
                for b in range(2):
                    stage_free(i, b)
                    for n in range(NBLK):
                        whole = min(BLK, T - n * BLK)
                        s.activation(
                            stage[:, b, 0:T].rearrange("p (t k) -> p k t", t=L)[:, n * BLK // L:(n * BLK + whole) // L],
                            ps[:, 3 * b + n, 0:whole].rearrange("p (k t) -> p k t", t=L), ACT.Copy)
                    s.activation(stage[:, b, T:N].rearrange("p (t b) -> p b t", t=TS),
                                 ps[:, 3 * b + 2, T - 2 * BLK:BLK].rearrange("p (b t) -> p b t", t=TS),
                                 ACT.Copy).then_inc(mm_free[b], 1)
                    store(i, b, t["u_d"][(2 * i + b) * P:(2 * i + b + 1) * P])
            for first, tiles, dst, func in ((T_U // 2, T_KEEP // 2, t["keep"], ACT.Copy),
                                            ((T_U + T_KEEP) // 2, T_GATE // 2, t["gate_d"], ACT.Sigmoid)):
                dst = dst.rearrange("(i b) p k -> i b p k", b=2)
                with act.Fori(0, tiles) as i:
                    for b in range(2):
                        stage_free(i + first, b)
                        s.activation(blocks(stage[:, b]), pset(b), func).then_inc(mm_free[b], 1)
                        store(i + first, b, dst[bass.ds(i, 1), b].rearrange("a p k -> p (a k)"))

            act.wait_ge(p5, 1)
            s.activation(wtt[:, 0], ps[:, 0:4, :].rearrange("p b (j m) -> p (b j) m", m=P), ACT.Copy).then_inc(a5, 1)
            act.wait_ge(p5, 2)
            s.activation(kpad[:].rearrange("c (j a) x -> c a j x", a=2)[:, 0, :, 7 * GC:],
                         ps[0:GC, 0:4, :].rearrange("p b (j m) -> p (b j) m", m=P), ACT.Copy).then_inc(a5, 1)
            act.wait_ge(p5, 5)
            s.activation(yg[:, 0:G:2], ps[:, 0:4, :].rearrange("p b (j m) -> p (b j) m", m=P), ACT.Copy).then_inc(a5, 1)

            def lru_acts(i):
                for b in range(2):
                    z = lru[b]
                    n = 2 * i + b
                    wait(act, lru_mm, 2 * n + 1)
                    wait(act, lru_h, n - 1)
                    s.activation(blocks(z["r"][:]), pset(0), ACT.Sigmoid, bias=z["par"][:, 5:6]).then_inc(lru_sig, 1)
                    act.wait_ge(lru_mm, 2 * n + 2)
                    s.activation(blocks(z["i"][:]), pset(1), ACT.Sigmoid, bias=z["par"][:, 6:7]).then_inc(lru_sig, 1)
                    act.wait_ge(lru_sig, 3 * n + 2)
                    s.activation(z["t"][:], z["r"][:], ACT.Tanh, scale=z["k"][:, 0:1]).then_inc(lru_sig, 1)
                    wait(act, lru_u, n + 1)
                    s.activation(z["m"][:], z["u"][:], ACT.Sqrt).then_inc(lru_sq, 1)

            lru_acts(0)
            with act.Fori(1, T_XA // 2) as i:
                lru_acts(i)

            def at_acts(i):
                def exps(u):
                    h, q = u // KD, u % KD
                    p2, n = u % 2, P * (q + 1)
                    wait(act, at_nb, 32 * i + u + 1)
                    wait(act, at_t, GRAN * i + transposed(u - 2))
                    s.activation(pm[:, p2, 0:n], sm[:, p2, 0:n], ACT.Exp, bias=mx[:, p2, 1:2], scale=SCALE,
                                 accum_out=mx[:, p2, 2:3]).then_inc(at_p, 1)

                def copies(u):
                    for k, g in enumerate(P_GRAN[u]):
                        n = min(P * 4, P * (u % KD + 1) - k * 4 * P)
                        wait(act, at_t, GRAN * i + g + 1)
                        wait(act, at_pv, 32 * i + u - 1)
                        s.activation(pt[:, u % 2, 4 * k:4 * k + n // P].rearrange("p j m -> p (j m)"),
                                     ps[:, 4 + g % 2, 0:n], ACT.Copy).then_inc(at_pt, 1)

                def values(u):
                    for k, g in enumerate(V_GRAN[u]):
                        wait(act, at_t, GRAN * i + g + 1)
                        wait(act, at_pv, 32 * i + u - 16)
                        s.activation(vn[:, u // 16, 4 * k:4 * k + 4].rearrange("p j m -> p (j m)"),
                                     ps[:, 4 + g % 2, :], ACT.Copy).then_inc(at_pt, 1)

                def outputs(u):
                    if u % 4 == 3:
                        h, half = u // KD, u % KD // 4
                        rows = slice(HD * (h % 2), HD * (h % 2) + HD)
                        wait(act, at_pv, 32 * i + u + 1)
                        wait(act, yo_out[h // 2], 16 * i)
                        s.activation(yo[rows, h // 2, 512 * half:512 * half + 512], ps[rows, 6 + u // 4 % 2, :],
                                     ACT.Copy).then_inc(at_o, 1)

                for x in range(-1, 33):
                    if x + 1 < 32:
                        if (x + 1) % 16 == 0:
                            values(x + 1)
                        exps(x + 1)
                    if 0 <= x < 32:
                        copies(x)
                    if x >= 1:
                        outputs(x - 1)

            at_acts(0)
            with act.Fori(1, HP // 2) as i:
                at_acts(i)

            def sa_acts(i):
                for b in range(2):
                    n = 2 * i + b
                    wait(act, sa_nb, n + 1)
                    wait(act, sa_t, n - 1)
                    s.activation(pms[:, b], sms[:, b], ACT.Exp, bias=mxs[:, b, 1:2], scale=SCALE,
                                 accum_out=mxs[:, b, 2:3]).then_inc(sa_p, 1)
                    wait(act, sa_t, n + 1)
                    wait(act, sa_pv, n - 1)
                    s.activation(pts[:, b, 0:KT].rearrange("p j m -> p (j m)"), ps[:, 4 + b, 0:KT * HQ], ACT.Copy)
                    s.activation(pts[0:NS, b, KT], ps[0:NS, 4 + b, KT * HQ:(KT + 1) * HQ], ACT.Copy).then_inc(sa_pt, 1)

            act.wait_ge(sa_vt, 1)
            s.activation(vnew[:].rearrange("p h m -> p (h m)"), ps[0:NS, 0:2, 0:384], ACT.Copy).then_inc(sa_vn, 1)
            sa_acts(0)
            with act.Fori(1, NB // 2) as i:
                sa_acts(i)

            for k in range(K_B):
                act.wait_ge(op_in[k % 2], 16 * (k // 2 + 1))
                wait(act, op_l, k)
                s.activation(prod_t[:, 0, 0:T].rearrange("p (k t) -> p t k", t=L),
                             stage[:, k % 2, 0:T].rearrange("p (t k) -> p t k", t=L), ACT.Gelu_apprx_tanh)
                s.activation(prod_t[:, 0, T:N].rearrange("p (b t) -> p t b", t=TS),
                             stage[:, k % 2, T:N].rearrange("p (t b) -> p t b", t=TS), ACT.Gelu_apprx_tanh).then_inc(g_act, 1)
                act.wait_ge(g_act, k + 1)
                s.activation(op_hi[:, k], prod_t[:, 0], ACT.Copy).then_inc(op_h, 1)
            for n in range(K_B):
                act.wait_ge(mm_ready[1], USES[P_GLU] + n + 1)
                wait(act, glu_y, n)
                s.activation(blocks(prod_t[:, 0]), pset(1), ACT.Sigmoid, bias=glu_b[:, 1, n:n + 1]).then_inc(mm_free[1], 1)
                act.wait_ge(glu_y, n + 1)
                s.activation(op_hi[:, K_B + n], prod_t[:, 1], ACT.Copy).then_inc(glu_h, 1)

            def operand(dst, first, k):
                act.wait_ge(op_in[k % 2], 16 * ((first + 1) // 2 + k // 2 + 1))
                s.activation(dst[:, k], stage[:, k % 2], ACT.Copy).then_inc(op_h, 1)

            for k in range(K_A):
                operand(hid_hi, K_B, k)
            act.wait_ge(merged, KD)
            for k in range(K_C):
                operand(op_hi, K_B + K_A, k)
            act.wait_ge(mm_ready[1], USES[P_OUT])
            act.wait_ge(mm_ready[0], USES[P_OUT])
            for k in range(KD):
                act.wait_ge(merged, 2 * KD + k + 1)
                s.activation(op_hi[:, k], acc[:, k], ACT.Copy).then_inc(o_hi, 1)
            def o_tile(k):
                b, u = k % 2, USES[P_OUT] + k // 2
                act.wait_ge(mm_ready[b], u + 1)
                act.wait_ge(o_lo, KD)
                s.activation(blocks(acc[:, k]), pset(b), ACT.Copy).then_inc(mm_free[b], 1)
                act.wait_ge(mm_free[b], u + 1)

            squares(n_mix, acc, o_tile)
            root(n_mix)
            squares(n_pre, resid, lambda k: act.wait_ge(x2_done, k + 1))
            root(n_pre)
            high_parts(n_pre)

            def hidden(tile, c, n, uses, parity):
                b = n % 2
                wait(act, mm_ready[b], uses + n // 2 + 1)
                wait(act, sq_done, tile)
                s.activation(blocks(stage[:, 0]), pset(b), ACT.Relu).then_inc(mm_free[b], 1)
                wait(act, sq_done, tile + 1)
                s.activation(hid_hi[:, FCH * parity + n], stage[:, 1], ACT.Copy).then_inc(hid_h, 1)

            act.wait_ge(x2_out, 16 * KD)
            act.wait_ge(n_pre.lo, KD)
            for n in range(FCH):
                hidden(n, 0, n, USES[P_MLP], 0)
            per = USES[P_MLP + 6] - USES[P_MLP + 2]
            with act.Fori(0, (NCH - 2) // 2) as c2:
                for c in range(2):
                    for n in range(FCH):
                        hidden(c2 * (2 * FCH) + (FCH * (c + 1) + n), None, n, c2 * (2 * per) + (c * per + USES[P_MLP + 2]),
                               (c + 1) % 2)
            for n in range(FCH):
                hidden(FCH * (NCH - 1) + n, None, n, USES[P_MLP + 2] + (NCH - 2) * per, 1)
            act.wait_ge(mm_free[0], USES[-1])
            act.wait_ge(mm_free[1], USES[-1])
            squares(n_ff, acc, lambda k: act.wait_ge(x2_in, 16 * KD))
            root(n_ff)

        @block.vector
        def _(dve):
            step = Steps(dve, dve_own)

            def tt(out, a, b, op):
                step(v.tensor_tensor(out, a, b, op))

            def ts(out, a, x, op, y=None, op2=None):
                step(v.tensor_scalar(out, a, x, y, op, op2) if op2 else v.tensor_scalar(out, a, x, None, op))

            def add_squares(n):
                for k in range(KD):
                    dve.wait_ge(n.sq, k + 1)
                    wait(dve, n.added, k)
                    if k == 0:
                        v.tensor_copy(n_sum[:], n_sq[:, 0]).then_inc(n.added, 1)
                    else:
                        v.tensor_tensor(n_sum[:], n_sum[:], n_sq[:, k % 2], ALU.add).then_inc(n.added, 1)

            def inverse_root(n):
                dve.wait_ge(n.rs, 1)
                step(v.reciprocal(n_rstd[:], n_rs[:]))

            def normed_parts(n, src, gain):
                for k in range(KD + 1):
                    if k < KD:
                        wait(dve, n.lo, k - 1)
                        v.scalar_tensor_tensor(out=n_tmp[:, k % 2], in0=src[:, k], scalar=gains[:, gain, k:k + 1],
                                               in1=n_rstd[:], op0=ALU.mult, op1=ALU.mult).then_inc(n.h, 1)
                    if k:
                        dve.wait_ge(n.hi, k)
                        v.tensor_tensor(op_lo[:, k - 1], n_tmp[:, (k - 1) % 2], op_hi[:, k - 1].bitcast(F32),
                                        ALU.subtract).then_inc(n.lo, 1)

            def add_normed(n, gain, done):
                for k in range(KD):
                    step(v.scalar_tensor_tensor(out=n_tmp[:, 0], in0=acc[:, k], scalar=gains[:, gain, k:k + 1],
                                                in1=n_rstd[:], op0=ALU.mult, op1=ALU.mult))
                    v.tensor_tensor(resid[:, k], resid[:, k], n_tmp[:, 0], ALU.add).then_inc(done, 1)
                    dve.wait_ge(done, k + 1)

            dve.wait_ge(const_in, 80)
            v.scalar_tensor_tensor(out=sp[:, 0], in0=lam[:], scalar=-1.0, in1=lam[:], op0=ALU.mult,
                                   op1=ALU.max).then_inc(lam_a, 1)
            dve.wait_ge(lam_e, 1)
            ts(sp[:, 2], sp[:, 1], 2.0, ALU.add)
            step(v.reciprocal(sp[:, 2], sp[:, 2]))
            tt(sp[:, 1], sp[:, 1], sp[:, 2], ALU.mult)
            tt(sp[:, 2], sp[:, 1], sp[:, 1], ALU.mult)
            ts(sp[:, 3], sp[:, 2], 1.0 / 17, ALU.mult)
            for n in range(15, 1, -2):
                step(v.scalar_tensor_tensor(out=sp[:, 3], in0=sp[:, 3], scalar=1.0 / n, in1=sp[:, 2], op0=ALU.add, op1=ALU.mult))
            step(v.scalar_tensor_tensor(out=sp[:, 3], in0=sp[:, 3], scalar=1.0, in1=sp[:, 1], op0=ALU.add, op1=ALU.mult))
            ts(sp[:, 4], lam[:], -1.0, ALU.mult, 0.0, ALU.max)
            step(v.scalar_tensor_tensor(out=sp[:, 3], in0=sp[:, 3], scalar=2.0, in1=sp[:, 4], op0=ALU.mult, op1=ALU.add))
            ts(lru_k[:], sp[:, 3], -4.0, ALU.mult)

            add_squares(n_in)
            inverse_root(n_in)
            normed_parts(n_in, acc, 0)

            def tiny(k):
                return s5_t[:, k]

            def wide(x, n):
                return x.unsqueeze(2).broadcast_to([P, J, n])

            def cmul(o, a, b, t1, t2, conj=False, negate_im=False):
                tt(t1, a[0], b[0], ALU.mult)
                tt(t2, a[1], b[1], ALU.mult)
                tt(o[0], t1, t2, ALU.add if conj else ALU.subtract)
                tt(t1, a[0], b[1], ALU.mult)
                tt(t2, a[1], b[0], ALU.mult)
                if negate_im:
                    step(v.scalar_tensor_tensor(out=o[1], in0=t1, scalar=-1.0, in1=t2, op0=ALU.mult, op1=ALU.subtract))
                else:
                    tt(o[1], t1, t2, ALU.subtract if conj else ALU.add)

            def from_tanh(o, th, t1):
                ts(t1, th, -1.0, ALU.mult, 1.0, ALU.add)
                step(v.reciprocal(t1, t1))
                step(v.scalar_tensor_tensor(out=o, in0=th, scalar=1.0, in1=t1, op0=ALU.add, op1=ALU.mult))

            def unit(re, im, t1, t2):
                tt(t1, re, re, ALU.mult)
                tt(t2, im, im, ALU.mult)
                tt(t1, t1, t2, ALU.add)
                ts(t1, t1, -0.5, ALU.mult, 1.5, ALU.add)
                tt(re, re, t1, ALU.mult)
                tt(im, im, t1, ALU.mult)

            lr, li = s5_in[:, 0], s5_in[:, 1]
            dve.wait_ge(s5_par_in, 48)
            dve.wait_ge(a5, 1)
            from_tanh(tiny(1), tiny(0), tiny(20))
            for _ in range(3):
                tt(tiny(1), tiny(1), tiny(1), ALU.mult)
            tt(tiny(2), lr, tiny(1), ALU.mult)
            tt(tiny(7), li, tiny(1), ALU.mult)
            ts(tiny(8), tiny(7), 1.0 / (2 * np.pi), ALU.mult)
            ts(tiny(8), tiny(8), ROUND, ALU.add)
            ts(tiny(8), tiny(8), ROUND, ALU.subtract)
            for part in (TWO_PI_HI, TWO_PI_MID, TWO_PI_LO):
                step(v.scalar_tensor_tensor(out=tiny(7), in0=tiny(8), scalar=-part, in1=tiny(7), op0=ALU.mult, op1=ALU.add))
            v.tensor_scalar(tiny(3), tiny(7), 3.1415925, -3.1415925, ALU.min, ALU.max).then_inc(d5p, 1)
            dve.wait_ge(a5, 4)
            dve.wait_ge(d5p, 1)
            from_tanh(tiny(9), tiny(4), tiny(20))
            tt(tiny(10), tiny(6), tiny(6), ALU.mult)
            ts(tiny(10), tiny(10), -2.0, ALU.mult, 1.0, ALU.add)
            step(v.tensor_copy(tiny(11), tiny(5)))
            unit(tiny(10), tiny(11), tiny(20), tiny(21))
            step(v.memset(pw[:, 0, :, 0:1], 1.0))
            step(v.memset(pw[:, 1, :, 0:1], 0.0))
            for k in range(2):
                tt(pw[:, k, :, 1], tiny(9), tiny(10 + k), ALU.mult)
            t1, t2 = (t5[:, k, :].rearrange("p (j k) -> p j k", j=J) for k in range(2))
            for n in (1, 2, 4):
                cmul([pw[:, k, :, n + 1:2 * n + 1] for k in range(2)], [pw[:, k, :, 1:n + 1] for k in range(2)],
                     [wide(pw[:, k, :, n], n) for k in range(2)], t1[:, :, 0:n], t2[:, :, 0:n])
            for n in range(L):
                step(v.tensor_copy(pwr[:, :, :, n], pw[:, :, :, L - 1 - n]))
            step(v.tensor_copy(tiny(12), tiny(9)))
            for _ in range(3):
                tt(tiny(12), tiny(12), tiny(12), ALU.mult)
            step(v.tensor_copy(dec[:], wide(tiny(12), C)))
            step(v.memset(dec[:, :, 0:1], 0.0))
            m, m2 = [tiny(10), tiny(11)], [tiny(13), tiny(14)]
            for _ in range(3):
                cmul(m2, m, m, tiny(20), tiny(21))
                m, m2 = m2, m
            unit(m[0], m[1], tiny(20), tiny(21))
            step(v.memset(ph[:, 0, :, 0:1], 1.0))
            step(v.memset(ph[:, 1, :, 0:1], 0.0))
            n = 1
            while n < C:
                cmul([ph[:, k, :, n:2 * n] for k in range(2)], [ph[:, k, :, 0:n] for k in range(2)],
                     [wide(m[k], n) for k in range(2)], t1[:, :, 0:n], t2[:, :, 0:n])
                n *= 2
                if n < C:
                    cmul(m2, m, m, tiny(20), tiny(21))
                    m, m2 = m2, m
                    unit(m[0], m[1], tiny(20), tiny(21))
            ts(tiny(15), pw[:, 0, :, 1], -1.0, ALU.add)
            ai = pw[:, 1, :, 1]
            tt(tiny(16), tiny(15), lr, ALU.mult)
            tt(tiny(17), ai, li, ALU.mult)
            tt(tiny(16), tiny(16), tiny(17), ALU.add)
            tt(tiny(17), ai, lr, ALU.mult)
            tt(tiny(18), tiny(15), li, ALU.mult)
            tt(tiny(17), tiny(17), tiny(18), ALU.subtract)
            tt(tiny(18), lr, lr, ALU.mult)
            tt(tiny(19), li, li, ALU.mult)
            tt(tiny(18), tiny(18), tiny(19), ALU.add)
            step(v.reciprocal(tiny(18), tiny(18)))
            tt(tiny(16), tiny(16), tiny(18), ALU.mult)
            tt(tiny(17), tiny(17), tiny(18), ALU.mult)
            cmul([bb[:, 0], bb[:, 1]], [wide(tiny(16), GC), wide(tiny(17), GC)], [bc_in[:, 0, 0], bc_in[:, 0, 1]],
                 t1[:, :, 0:GC], t2[:, :, 0:GC])
            for n in range(L):
                cmul([wt[:, 0, :, n], wt[:, 1, :, n]], [wide(pwr[:, k, :, n], GC) for k in range(2)], [bb[:, 0], bb[:, 1]],
                     t1[:, :, 0:GC], t2[:, :, 0:GC])
            for n in range(L + 1):
                cmul([rx[:, 0, :, n], rx[:, 1, :, n]], [wide(pw[:, k, :, n], GC) for k in range(2)],
                     [bc_in[:, 1, 0], bc_in[:, 1, 1]], t1[:, :, 0:GC], t2[:, :, 0:GC], negate_im=True)
            step(v.memset(st[:, :, :, 0:1], 0.0))
            v.memset(s5_t[:, 22:24], 0.0).then_inc(d5, 1)

            dve.wait_ge(p5, 1)
            v.tensor_copy(wtt[:, 1], ps[:, 4:8, :].rearrange("p b (j m) -> p (b j) m", m=P)).then_inc(d5, 1)
            step(v.memset(kpad[:, :, 0:7 * GC], 0.0))
            dve.wait_ge(p5, 2)
            step(v.tensor_copy(kpad[:].rearrange("c (j a) x -> c a j x", a=2)[:, 1, :, 7 * GC:],
                               ps[0:GC, 4:8, :].rearrange("p b (j m) -> p (b j) m", m=P)))
            diag = t5[0:GC, 0, 0:G * GC].rearrange("p (g c) -> p g c", g=G)
            tt(diag, s5_d[:].unsqueeze(2).broadcast_to([GC, G, GC]), ident[0:GC, 0:GC].unsqueeze(1).broadcast_to([GC, G, GC]), ALU.mult)
            dve.wait_ge(a5, 6)
            now = kpad[:, :, 7 * GC:8 * GC]
            v.tensor_tensor(now, now, diag, ALU.add).then_inc(d5, 1)
            for b in range(2):
                dve.wait_ge(stored[b], 16 * (T_IN // 2))
            v.memset(us, 0.0).then_inc(d5, 1)
            dve.wait_ge(p5, 3)
            vps = [ps[:, 4 * k:4 * k + 4, :].rearrange("p b (j m) -> p (b j) m", m=C) for k in range(2)]
            cmul([z5[:, 0], z5[:, 1]], [ph[:, 0], ph[:, 1]], vps, t1, t2, conj=True)
            flat_dec = dec[:].rearrange("p j k -> p (j k)")
            for k in range(2):
                ins = v.tensor_tensor_scan(out=t5[:, k], data0=flat_dec, data1=z5[:, k].rearrange("p j k -> p (j k)"),
                                           initial=0.0, op0=ALU.mult, op1=ALU.add)
                if k == 0:
                    ins.then_inc(d5, 1)
                else:
                    step(ins)
            dve.wait_ge(d5, 5)
            cmul([st[:, 0, :, 1:], st[:, 1, :, 1:]], [ph[:, 0], ph[:, 1]], [t1, t2], z5[:, 0], z5[:, 1])
            step(v.tensor_copy(p_fin[:], st[:, :, :, C]))
            v.memset(s5_t[:, 22:24], 0.0).then_inc(d5, 1)
            dve.wait_ge(p5, 4)
            dve.wait_ge(s0_in, 16)
            vs = [ps[:, 0, k * J * NB:(k + 1) * J * NB].rearrange("p (j b) -> p j b", j=J) for k in range(2)]
            cmul([sq[:, 0], sq[:, 1]], [wide(pw[:, k, :, TS], NB) for k in range(2)], [s0[:, 0], s0[:, 1]],
                 sq[:, 2], sq[:, 3])
            tt(sf[:, 0], sq[:, 0], vs[0], ALU.add)
            tt(sf[:, 1], sq[:, 1], vs[1], ALU.add)
            v.tensor_copy(ys.rearrange("p (j a) b -> p j a b", a=2),
                          ps[:, 1:3, 0:J * NB].rearrange("p a (j b) -> p j a b", b=NB)).then_inc(d5, 1)
            v.memset(s5_t[:, 22:24], 0.0).then_inc(d5, 1)
            dve.wait_ge(p5, 5)
            v.tensor_copy(yg[:, 1:G:2], ps[:, 4:8, :].rearrange("p b (j m) -> p (b j) m", m=P)).then_inc(d5, 1)

            def lru_tile(i, b):
                z, n = lru[b], 2 * i + b
                par = z["par"]
                dve.wait_ge(lru_in[b], 80 * (i + 1))
                step(v.tensor_copy(z["k"][:], lru_k[:, bass.ds(i * 2 + b, 1)] if not isinstance(i, int) else lru_k[:, n:n + 1]))
                for x, out in ((z["x"], z["xc"][:, 0:T]), (z["xs"], z["xc"][:, T:N].rearrange("p (b t) -> p b t", b=NB))):
                    for k in range(CW):
                        src = x[:, k:k + T] if x is z["x"] else x[:, :, k:k + TS]
                        if k == 0:
                            ts(out, src, par[:, 0:1], ALU.mult, par[:, 4:5], ALU.add)
                        elif k < CW - 1 or x is z["x"]:
                            step(v.scalar_tensor_tensor(out=out, in0=src, scalar=par[:, k:k + 1], in1=out, op0=ALU.mult, op1=ALU.add))
                        else:
                            v.scalar_tensor_tensor(out=out, in0=src, scalar=par[:, k:k + 1], in1=out, op0=ALU.mult,
                                                   op1=ALU.add).then_inc(lru_xc, 1)
                dve.wait_ge(lru_xc, n + 1)
                dve.wait_ge(lru_sig, 3 * n + 3)
                v.tensor_scalar(z["u"][:], z["t"][:], -1.0, TINY, ALU.mult, ALU.max).then_inc(lru_u, 1)
                ts(z["r"][:], z["t"][:], -1.0, ALU.mult, 1.0, ALU.add)
                step(v.reciprocal(z["q"][:], z["r"][:]))
                ts(z["a"][:], z["q"][:], 2.0, ALU.mult, -1.0, ALU.add)
                tt(z["i"][:], z["i"][:], z["xc"][:], ALU.mult)
                dve.wait_ge(lru_sq, n + 1)
                step(v.scalar_tensor_tensor(out=z["b"][:], in0=z["m"][:], scalar=2.0, in1=z["q"][:], op0=ALU.mult, op1=ALU.mult))
                tt(z["b"][:], z["b"][:], z["i"][:], ALU.mult)
                a0, b0 = z["a"][:, T:N:TS], z["b"][:, T:N:TS]
                tt(z["h0"][:], a0, par[:, 8:16], ALU.mult)
                tt(b0, b0, z["h0"][:], ALU.add)
                step(v.memset(a0, 0.0))
                wait(dve, lru_stored[b], 16 * i)
                v.tensor_tensor_scan(out=z["h"][:], data0=z["a"][:], data1=z["b"][:], initial=0.0,
                                     op0=ALU.mult, op1=ALU.add).then_inc(lru_h, 1)
                dve.wait_ge(lru_h, n + 1)

            def lru_round(i):
                for b in range(2):
                    lru_tile(i, b)

            for b in range(2):
                dve.wait_ge(lru_in[b], 80)
                step(v.memset(lru[b]["x"][:, 0:CW - 1], 0.0))
            step.repeat(T_XA // 2, lru_round)

            dve.wait_ge(bias_in, 16)

            def at_round(i):
                def maxima(u):
                    q, p2, n = u % KD, u % 2, P * (u % KD + 1)
                    dve.wait_ge(at_s, UNITS * i + u + 1)
                    wait(dve, at_p, UNITS * i + u - 1)
                    dve.sem_inc(go, 1)
                    v.tensor_tensor_reduce(sm[:, p2, 0:n], ps[:, 2 * p2:2 * p2 + 2, :].rearrange("p b n -> p (b n)")[:, 0:n],
                                           bias[:, T - n:T], 1.0, MASKED * 2, ALU.add, ALU.max,
                                           mx[:, p2, 0:1]).then_inc(at_masked, 1)
                    dve.wait_ge(at_masked, UNITS * i + u + 1)
                    v.tensor_scalar(mx[:, p2, 1:2], mx[:, p2, 0:1], -SCALE, None, ALU.mult).then_inc(at_nb, 1)

                def normed(u):
                    p2, n = u % 2, P * (u % KD + 1)
                    dve.wait_ge(at_p, UNITS * i + u + 1)
                    step(v.reciprocal(mx[:, p2, 3:4], mx[:, p2, 2:3]))
                    v.tensor_scalar(pm[:, p2, 0:n], pm[:, p2, 0:n], mx[:, p2, 3:4], None, ALU.mult).then_inc(at_pn, 1)

                for x in range(-1, UNITS):
                    if x >= 0:
                        normed(x)
                    if x + 1 < UNITS:
                        maxima(x + 1)

            step.repeat(HP // 2, at_round)

            step(v.memset(sqd[:], 0.0))
            dve.wait_ge(qkvs_in, 48)
            for h in range(HEADS):
                rows = slice(HD * (h % 2), HD * (h % 2) + HD)
                step(v.tensor_copy(sqd[rows, h // 2, :, h * TS:(h + 1) * TS],
                                   qkvs[rows, 0, h // 2].rearrange("p (b t) -> p b t", b=NB)))

            def sa_round(i):
                for b in range(2):
                    n = 2 * i + b
                    wait(dve, sa_s, n - 1)
                    src = sqd[:].rearrange("p h (i b) m -> p h i b m", b=2)
                    src = src[:, :, i, b] if isinstance(i, int) else src[:, :, bass.ds(i, 1), b].rearrange("p h a m -> p h (a m)")
                    v.tensor_copy(sq1[:, b], src).then_inc(sa_q1, 1)
                    dve.wait_ge(sa_s, n + 1)
                    dve.wait_ge(kv_in[b], 48 * (i + 1))
                    wait(dve, sa_p, n - 1)
                    dve.sem_inc(go, 1)
                    v.tensor_tensor_reduce(sms[:, b], ps[0:HQ, 2 * b:2 * b + 2, :].rearrange("p b n -> p (b n)")[:, 0:NK],
                                           sbias[:, b], 1.0, MASKED * 2, ALU.add, ALU.max, mxs[:, b, 0:1]).then_inc(sa_masked, 1)
                    dve.wait_ge(sa_masked, n + 1)
                    v.tensor_scalar(mxs[:, b, 1:2], mxs[:, b, 0:1], -SCALE, None, ALU.mult).then_inc(sa_nb, 1)
                    dve.wait_ge(sa_p, n + 1)
                    step(v.reciprocal(mxs[:, b, 3:4], mxs[:, b, 2:3]))
                    v.tensor_scalar(pms[:, b], pms[:, b], mxs[:, b, 3:4], None, ALU.mult).then_inc(sa_pn, 1)
                    dve.wait_ge(sa_pv, n + 1)
                    for h in range(2):
                        rows = slice(HD * h, HD * h + HD)
                        out = yos[rows].rearrange("p h (i b) t -> p h i b t", b=2)
                        out = out[:, :, i, b] if isinstance(i, int) else out[:, :, bass.ds(i, 1), b].rearrange("p h a t -> p h (a t)")
                        src = ps[rows, 6 + b, 0:HP * 2 * TS].rearrange("p (h m) -> p h m", m=2 * TS)[:, :, h * TS:(h + 1) * TS]
                        ins = v.tensor_copy(out, src)
                    ins.then_inc(sa_o, 1)

            step.repeat(NB // 2, sa_round)

            for k in range(K_B):
                dve.wait_ge(op_h, k + 1)
                v.tensor_tensor(op_lo[:, k], prod_t[:, 0], op_hi[:, k].bitcast(F32), ALU.subtract).then_inc(op_l, 1)
            for n in range(K_B):
                dve.wait_ge(mm_ready[0], USES[P_GLU] + n + 1)
                dve.wait_ge(mm_free[1], USES[P_GLU] + n + 1)
                wait(dve, glu_l, n)
                v.scalar_tensor_tensor(out=blocks(prod_t[:, 1]), in0=pset(0), scalar=glu_b[:, 0, n:n + 1],
                                       in1=blocks(prod_t[:, 0]), op0=ALU.add, op1=ALU.mult).then_inc(glu_y, 1)
                dve.wait_ge(glu_y, n + 1)
                dve.sem_inc(mm_free[0], 1)
                dve.wait_ge(glu_h, n + 1)
                v.tensor_tensor(op_lo[:, K_B + n], prod_t[:, 1], op_hi[:, K_B + n].bitcast(F32), ALU.subtract).then_inc(glu_l, 1)
            for k in range(K_A):
                dve.wait_ge(op_h, K_B + k + 1)
                v.tensor_tensor(hid_lo[:, k], stage[:, k % 2], hid_hi[:, k].bitcast(F32), ALU.subtract).then_inc(op_l, 1)
            dve.wait_ge(glu_l, K_B)
            for n in range(KD):
                b = n % 2
                dve.wait_ge(mm_ready[b], USES[P_B] + n // 2 + 1)
                dve.wait_ge(gate_in[b], 16 * (n // 2 + 1))
                v.tensor_tensor(blocks(acc[:, n]), pset(b), blocks(gate_t[:, b]), ALU.mult).then_inc(merged, 1)
                dve.wait_ge(merged, n + 1)
                dve.sem_inc(mm_free[b], 1)

            def add_branch(first_pair, done):
                def tiles(i):
                    for b in range(2):
                        n = 2 * i + b
                        dve.wait_ge(mm_ready[b], USES[first_pair] + 1 + i)
                        dve.wait_ge(gate_in[b], 16 * (done // 2 + 1) + 16 * i)
                        v.tensor_tensor(blocks(prod_t[:, b]), pset(b), blocks(gate_t[:, b]), ALU.mult).then_inc(mm_free[b], 1)
                        dve.wait_ge(mm_free[b], USES[first_pair] + 1 + i)
                        a = acc[:].rearrange("p (i b) n -> p i b n", b=2)
                        a = a[:, i, b] if isinstance(i, int) else a[:, bass.ds(i, 1), b].rearrange("p a n -> p (a n)")
                        v.tensor_tensor(a, a, prod_t[:, b], ALU.add).then_inc(merged, 1)
                        dve.wait_ge(merged, n + (done + 1))
                step.repeat(KD // 2, tiles)

            for k in range(K_C):
                dve.wait_ge(op_h, K_B + K_A + k + 1)
                v.tensor_tensor(op_lo[:, k], stage[:, k % 2], op_hi[:, k].bitcast(F32), ALU.subtract).then_inc(op_l, 1)
            add_branch(P_A, KD)
            add_branch(P_C, 2 * KD)
            for k in range(KD):
                dve.wait_ge(o_hi, k + 1)
                v.tensor_tensor(op_lo[:, k], acc[:, k], op_hi[:, k].bitcast(F32), ALU.subtract).then_inc(o_lo, 1)

            add_squares(n_mix)
            inverse_root(n_mix)
            dve.wait_ge(x_again, 16 * KD)
            add_normed(n_mix, 1, x2_done)
            step(v.memset(acc[:], 0.0))
            add_squares(n_pre)
            inverse_root(n_pre)
            normed_parts(n_pre, resid, 2)

            def hidden(tile, n, parity):
                b = n % 2
                wait(dve, mm_free[b], tile[1] + n // 2 + 1)
                v.tensor_tensor(stage[:, 1], stage[:, 0], stage[:, 0], ALU.mult).then_inc(sq_done, 1)
                dve.wait_ge(hid_h, tile[0] + 1)
                v.tensor_tensor(hid_lo[:, FCH * parity + n], stage[:, 1], hid_hi[:, FCH * parity + n].bitcast(F32),
                                ALU.subtract).then_inc(hid_l, 1)
                dve.wait_ge(hid_l, tile[0] + 1)

            def sums(uses):
                for n in range(KD):
                    b = n % 2
                    dve.wait_ge(mm_ready[b], uses + (n // 2 + 1))
                    v.tensor_tensor(blocks(acc[:, n]), blocks(acc[:, n]), pset(b), ALU.add).then_inc(mm_free[b], 1)

            dve.wait_ge(x2_out, 16 * KD)
            dve.wait_ge(n_pre.lo, KD)
            for n in range(FCH):
                hidden((n, USES[P_MLP]), n, 0)
            per = USES[P_MLP + 6] - USES[P_MLP + 2]
            u1 = USES[P_MLP + 2]
            with dve.Fori(0, (NCH - 2) // 2) as c2:
                for c in range(2):
                    for n in range(FCH):
                        hidden((c2 * (2 * FCH) + (FCH * (c + 1) + n), c2 * (2 * per) + (c * per + u1)), n, (c + 1) % 2)
                    sums(c2 * (2 * per) + (c * per + u1 + 2))
            last = u1 + (NCH - 2) * per
            for n in range(FCH):
                hidden((FCH * (NCH - 1) + n, last), n, 1)
            sums(last + 2)
            sums(last + per)
            add_squares(n_ff)
            inverse_root(n_ff)
            dve.wait_ge(x2_in, 16 * KD)
            add_normed(n_ff, 3, y_done)

        @block.tensor
        def _(te):
            def product(i, b, kts, dst, w0, hi, lo, ready, uses):
                wait(te, w_split[b], i + 1)
                wait(te, mm_free[dst], uses)
                for n, k in enumerate(kts):
                    ready(k)
                    for part, (w, x) in enumerate(((w_hi, hi), (w_hi, lo), (w_lo, hi))):
                        for q in range(NBLK):
                            mm = pe.matmul(ps[:, 3 * dst + q, 0:BLK], w[:, b, w0 + n], x[:, k, q * BLK:(q + 1) * BLK],
                                           start=(n == 0 and part == 0), stop=(n == len(kts) - 1 and part == 2))
                mm.then_inc(mm_ready[dst], 1)

            def nothing(k):
                pass

            def sum_squares(n, uses):
                te.wait_ge(n.added, KD)
                wait(te, mm_free[0], uses)
                for q in range(NBLK):
                    mm = pe.matmul(ps[:, q, 0:BLK], ones[:], n_sum[:, q * BLK:(q + 1) * BLK], start=True, stop=True)
                mm.then_inc(n.sum, 1)

            te.wait_ge(const_in, 80)
            sum_squares(n_in, 0)
            for b in range(2):
                product(0, b, range(KD), b, 0, op_hi, op_lo, lambda k: te.wait_ge(n_in.lo, k + 1), 0)
            with te.Fori(1, T_IN // 2) as i:
                for b in range(2):
                    product(i, b, range(KD), b, 0, op_hi, op_lo, nothing, i)

            te.wait_ge(d5, 1)
            for b in range(2):
                te.wait_ge(mm_free[b], T_IN // 2)
            for a in range(2):
                for j in range(J):
                    mm = pe.transpose(ps[:, 4 * a + j // 4, P * (j % 4):P * (j % 4) + P],
                                      wt[:, a, j].rearrange("p t c -> p (t c)"), ident[:])
            mm.then_inc(p5, 1)
            te.wait_ge(a5, 5)
            te.wait_ge(d5, 2)
            for a in range(2):
                rows = slice(NST * a, NST * a + NST)
                for j in range(J):
                    for part in range(2):
                        mm = pe.matmul(ps[0:GC, 4 * a + j // 4, P * (j % 4):P * (j % 4) + P], bb[rows, part, j],
                                       rx[rows, part, j, 0:L].rearrange("p t c -> p (t c)"),
                                       start=(part == 0), stop=(part == 1))
            mm.then_inc(p5, 1)
            te.wait_ge(ug_in, 16 * L)
            te.wait_ge(a5, 6)
            te.wait_ge(d5, 3)
            for g in range(G):
                j, a = g // 2, g % 2
                for part in range(2):
                    mm = pe.matmul(ps[NST * a:NST * a + NST, 4 * part + j // 4, C * (j % 4):C * (j % 4) + C],
                                   wtt[:, part, j, NST * a:NST * a + NST], ug[:, g], start=True, stop=True)
            mm.then_inc(p5, 1)
            te.wait_ge(us_in, 16 * 2 * TS)
            te.wait_ge(s0_in, 16)
            te.wait_ge(toep_in, 16 * L)
            te.wait_ge(d5, 5)
            for g in range(G):
                j, a = g // 2, g % 2
                rows = slice(NST * a, NST * a + NST)
                for part in range(2):
                    at0 = (part * J + j) * NB
                    pe.matmul(ps[rows, 0, at0:at0 + NB], wtt[:, part, j, rows], us[:, 1, g], start=True, stop=True)
                pe.matmul(ps[:, 1 + a, j * NB:(j + 1) * NB], toep[:, g], us[:, 0, g], start=True, stop=False)
                for part in range(2):
                    mm = pe.matmul(ps[:, 1 + a, j * NB:(j + 1) * NB], rx[rows, part, j, 1:].rearrange("p t c -> p (t c)"),
                                   s0[rows, part, j], start=False, stop=(part == 1))
            mm.then_inc(p5, 1)
            te.wait_ge(d5, 8)
            for g in range(G):
                j, a = g // 2, g % 2
                rows = slice(NST * a, NST * a + NST)
                out = ps[:, 4 * a + j // 4, C * (j % 4):C * (j % 4) + C]
                pe.matmul(out, toep[:, g], ug[:, g], start=True, stop=False)
                for part in range(2):
                    mm = pe.matmul(out, rx[rows, part, j, 1:].rearrange("p t c -> p (t c)"), st[rows, part, j, 0:C],
                                   start=False, stop=(part == 1))
            mm.then_inc(p5, 1)

            te.wait_ge(a5, 7)
            te.wait_ge(d5, 9)

            def lru_gates(i):
                for b in range(2):
                    z, n = lru[b], 2 * i + b
                    te.wait_ge(lru_xc, n + 1)
                    te.wait_ge(lru_in[b], 80 * (i + 1))
                    for a in range(2):
                        wait(te, lru_sig, 3 * n - 2 + a)
                        for q in range(NBLK):
                            mm = pe.matmul(ps[:, 3 * a + q, 0:BLK], z["w"][:, a], z["xc"][:, q * BLK:(q + 1) * BLK],
                                           start=True, stop=True)
                        mm.then_inc(lru_mm, 1)

            lru_gates(0)
            with te.Fori(1, T_XA // 2) as i:
                lru_gates(i)

            te.wait_ge(lru_sig, 3 * T_XA)

            def at_round(i):
                def scores(u):
                    h, q, p2, n = u // KD, u % KD, u % 2, P * (u % KD + 1)
                    rows = slice(HD * (h % 2), HD * (h % 2) + HD)
                    te.wait_ge(at_in[h // 2], 48 * (i + 1))
                    wait(te, at_masked, UNITS * i + u - 1)
                    for c in range(0, n, 512):
                        m = min(512, n - c)
                        mm = pe.matmul(ps[:, 2 * p2 + c // 512, 0:m], qkv[rows, h // 2, 0, P * q:P * q + P],
                                       qkv[rows, h // 2, 1, c:c + m], start=True, stop=True)
                    mm.then_inc(at_s, 1)

                def bank_free(g):
                    wait(te, at_pt, GRAN * i + g - 1)

                def values(u):
                    te.wait_ge(at_in[u // 16], 48 * (i + 1))
                    for k, g in enumerate(V_GRAN[u]):
                        bank_free(g)
                        for j in range(4):
                            mm = pe.transpose(ps[:, 4 + g % 2, P * j:P * j + P],
                                              qkv[:, u // 16, 2, P * (4 * k + j):P * (4 * k + j) + P], ident[:])
                        mm.then_inc(at_t, 1)

                def transposes(u):
                    te.wait_ge(at_pn, UNITS * i + u + 1)
                    for k, g in enumerate(P_GRAN[u]):
                        bank_free(g)
                        for j in range(min(4, u % KD + 1 - 4 * k)):
                            mm = pe.transpose(ps[:, 4 + g % 2, P * j:P * j + P],
                                              pm[:, u % 2, P * (4 * k + j):P * (4 * k + j) + P], ident[:])
                        mm.then_inc(at_t, 1)

                def outputs(u):
                    h, q = u // KD, u % KD
                    rows = slice(HD * (h % 2), HD * (h % 2) + HD)
                    te.wait_ge(at_pt, GRAN * i + P_GRAN[u][-1] + 1)
                    if q % 4 == 0:
                        wait(te, at_o, 8 * i + u // 4 - 1)
                    for j in range(q + 1):
                        mm = pe.matmul(ps[rows, 6 + u // 4 % 2, P * (q % 4):P * (q % 4) + P], vn[:, h // 2, j, rows],
                                       pt[:, u % 2, j], start=(j == 0), stop=(j == q))
                    mm.then_inc(at_pv, 1)

                for x in range(-1, UNITS + 1):
                    if x + 1 < UNITS:
                        if (x + 1) % (2 * KD) == 0:
                            values(x + 1)
                        scores(x + 1)
                    if 0 <= x < UNITS:
                        transposes(x)
                    if x >= 1:
                        outputs(x - 1)

            at_round(0)
            with te.Fori(1, HP // 2) as i:
                at_round(i)

            te.wait_ge(at_masked, UNITS * (HP // 2))
            te.wait_ge(at_pt, GRAN * (HP // 2))
            te.wait_ge(at_o, 8 * (HP // 2))
            te.wait_ge(qkvs_in, 48)
            for h in range(HP):
                mm = pe.transpose(ps[0:NS, h // 3, P * (h % 3):P * (h % 3) + P], qkvs[:, 2, h], ident[:])
            mm.then_inc(sa_vt, 1)
            te.wait_ge(sa_vn, 1)

            def sa_round(i):
                for b in range(2):
                    n = 2 * i + b
                    te.wait_ge(kv_in[b], 48 * (i + 1))
                    te.wait_ge(sa_q1, n + 1)
                    wait(te, sa_masked, n - 1)
                    for bank, lo, cols, keys in ((2 * b, 0, 512, kc[b][:, :, 0:512]),
                                                 (2 * b + 1, 0, NCK - 512, kc[b][:, :, 512:NCK]),
                                                 (2 * b + 1, NCK - 512, NS, qkvs[:, 1])):
                        for h in range(HP):
                            mm = pe.matmul(ps[0:HQ, bank, lo:lo + cols], sq1[:, b, h], keys[:, h],
                                           start=(h == 0), stop=(h == HP - 1))
                    mm.then_inc(sa_s, 1)
                    te.wait_ge(sa_pn, n + 1)
                    wait(te, sa_pt, n - 1)
                    te.sem_inc(go, 1)
                    for j in range(KT + 1):
                        m = P if j < KT else NS
                        mm = pe.transpose(ps[0:m, 4 + b, HQ * j:HQ * j + HQ], pms[:, b, P * j:P * j + m], ident[0:HQ, 0:HQ])
                    mm.then_inc(sa_t, 1)
                    te.wait_ge(sa_pt, n + 1)
                    wait(te, sa_o, n - 1)
                    for h in range(HP):
                        for j in range(KT + 1):
                            lhs = vc[b][:, j, P * h:P * h + P] if j < KT else vnew[:, h]
                            m = P if j < KT else NS
                            mm = pe.matmul(ps[:, 6 + b, 2 * TS * h:2 * TS * (h + 1)], lhs,
                                           pts[0:m, b, j, 2 * TS * h:2 * TS * (h + 1)], start=(j == 0), stop=(j == KT))
                    mm.then_inc(sa_pv, 1)

            sa_round(0)
            with te.Fori(1, NB // 2) as i:
                sa_round(i)
            te.wait_ge(sa_o, NB)

            for m in range(K_B):
                for dst in range(2):
                    product(P_GLU + m // 2, m % 2, range(K_B), dst, K_B * dst, op_hi, op_lo,
                            lambda k: te.wait_ge(op_l, k + 1), USES[P_GLU] + m)
            for m in range(KD // 2):
                for dst in range(2):
                    product(P_B + m // 2, m % 2, range(K_B, 2 * K_B), dst, K_B * dst, op_hi, op_lo,
                            lambda k: te.wait_ge(glu_l, k - K_B + 1), USES[P_B] + m)

            def projection(first, kts, hi, lo, ready):
                u0 = USES[first]
                for b in range(2):
                    product(first, b, kts, b, 0, hi, lo, ready, u0)
                with te.Fori(1, KD // 2) as i:
                    for b in range(2):
                        product(i + first, b, kts, b, 0, hi, lo, nothing, i + u0)

            projection(P_A, range(K_A), hid_hi, hid_lo, lambda k: te.wait_ge(op_l, K_B + k + 1))
            projection(P_C, range(K_C), op_hi, op_lo, lambda k: te.wait_ge(op_l, K_B + K_A + k + 1))
            projection(P_OUT, range(KD), op_hi, op_lo, lambda k: te.wait_ge(o_lo, k + 1))
            sum_squares(n_mix, USES[P_MLP])
            sum_squares(n_pre, 0)

            def up(pair, ready, uses):
                for n in range(FCH):
                    product(pair + n // 2, n % 2, range(KD), n % 2, 0, op_hi, op_lo,
                            ready, uses + n // 2)

            def down(pair, parity, hidden_tiles, uses):
                te.wait_ge(hid_l, hidden_tiles)
                for m in range(KD // 2):
                    for dst in range(2):
                        product(pair + m // 2, m % 2, range(FCH * parity, FCH * parity + FCH), dst, FCH * dst,
                                hid_hi, hid_lo, nothing, uses + m)

            up(P_MLP, lambda k: te.wait_ge(n_pre.lo, k + 1), USES[P_MLP])
            per, u1, p1 = USES[P_MLP + 6] - USES[P_MLP + 2], USES[P_MLP + 2], P_MLP + 2
            with te.Fori(0, (NCH - 2) // 2) as c2:
                for c in range(2):
                    up(c2 * 8 + (4 * c + p1), nothing, c2 * (2 * per) + (c * per + u1))
                    down(c2 * 8 + (4 * c + p1 + 2), c, c2 * (2 * FCH) + FCH * (c + 1), c2 * (2 * per) + (c * per + u1 + 2))
            c = NCH - 2
            up(p1 + 4 * c, nothing, u1 + c * per)
            down(p1 + 4 * c + 2, 0, FCH * (c + 1), u1 + c * per + 2)
            down(p1 + 4 * c + 4, 1, FCH * (c + 2), u1 + (c + 1) * per)
            sum_squares(n_ff, USES[-1])


def _features(a):
    n = a.shape[-1] // P
    return a.reshape(-1, n, P).transpose(2, 1, 0)


def _tiles(w):
    k, m = w.shape
    return w.reshape(k // P, P, m // P, P).transpose(2, 1, 0, 3)


def _doubled(tiles, first, second):
    return np.concatenate([tiles[first], tiles[second]], axis=2)


def _log_count(delta):
    count = sum(((delta >= 0) & (delta <= w) & (delta % d == 0)).astype(np.int64) for w, d in GROUPS)
    return np.where(count > 0, np.log(np.maximum(count, 1)) / SCALE, MASKED).astype(np.float32)


def kernel(**inputs):
    import concourse.bacc as bacc
    from concourse.bass_utils import run_bass_kernel_spmd

    a = {k: np.asarray(x)[0] if k not in ("x_prompt", "x_sample") else np.asarray(x) for k, x in inputs.items()}
    w_in = _tiles(a["w_in"])
    xa, u = slice(0, T_XA), slice(T_XA, T_XA + T_U)
    rest = slice(T_XA + T_U, None)
    glu, pb = _tiles(a["glu_w"]), _tiles(a["w_proj_b"])
    pad = np.zeros((KD, P, KD - K_A, P), np.float32)
    w1, w2 = _tiles(a["mlp_w1"]), [_tiles(a["mlp_w2"][c * FCH * P:(c + 1) * FCH * P]) for c in range(NCH)]
    even, odd = slice(0, None, 2), slice(1, None, 2)
    up = [w1[c * FCH:(c + 1) * FCH] for c in range(NCH)]
    down = [_doubled(w, even, odd) for w in w2]
    mlp = [up[0]]
    for c in range(NCH - 1):
        mlp += [up[c + 1], down[c]]
    mlp.append(down[-1])
    stream = np.concatenate([
        w_in[u], w_in[xa], w_in[rest], _doubled(glu, slice(0, K_B), slice(K_B, None)), _doubled(pb, even, odd),
        np.concatenate([_tiles(a["w_proj_a"]), pad], axis=2), np.concatenate([_tiles(a["w_proj_c"]), pad], axis=2),
        _tiles(a["w_out"])] + mlp)
    blocks = np.zeros((T_XA, P, 2, P), np.float32)
    for n, name in enumerate(("lru_wr", "lru_wi")):
        for h in range(2):
            half = slice(64 * h, 64 * h + 64)
            blocks[:, half, n, half] = a[name][h::2]
    par = np.zeros((T_XA, P, 16), np.float32)
    par[:, :, 0:CW] = a["conv_w"].reshape(CW, T_XA, P).transpose(1, 2, 0)
    par[:, :, 4] = a["conv_b"].reshape(T_XA, P)
    par[:, :, 5] = a["lru_br"].reshape(T_XA, P)
    par[:, :, 6] = a["lru_bi"].reshape(T_XA, P)
    par[:, :, 8:16] = a["state_lru"].reshape(NB, T_XA, P).transpose(1, 2, 0)

    def states(x):
        x = x.reshape((J, 2, NST) + x.shape[2:])
        return np.moveaxis(x, 0, 2).reshape((P, J) + x.shape[3:])

    rows = np.concatenate([np.arange(W_MAX - NEAR, W_MAX),
                           (np.arange(0, W_MAX - NEAR, 16)[:, None] + np.arange(TS)).ravel()])
    kc = a["cache_k"][:, rows].reshape(NB, NCK, HP, P).transpose(0, 3, 2, 1)
    vc = a["cache_v"][:, rows].reshape(NB, KT, P, AW).transpose(0, 2, 1, 3)
    q = np.arange(TS)
    old = _log_count(W_MAX + q[:, None] - rows[None, :])
    sbias = np.full((NB, HEADS, TS, NK), MASKED, np.float32)
    sbias[..., :NCK] = old
    for b in range(NB):
        sbias[b, :, :, NCK + b * TS:NCK + (b + 1) * TS] = _log_count(q[:, None] - q[None, :])
    arrays = dict(
        w=stream.reshape(-1, P, KD * P),
        x=np.concatenate([_features(a["x_prompt"]), _features(a["x_sample"])], axis=2),
        ident=np.eye(P, dtype=np.float32), ones=np.ones((P, P), np.float32),
        gains=np.stack([a[k].reshape(KD, P).T for k in ("norm_pre_mix", "norm_post_mix", "norm_pre_mlp", "norm_post_mlp")], 1),
        glu_b=a["glu_b"].reshape(2, K_B, P).transpose(2, 0, 1),
        lam=a["lru_lambda"].reshape(T_XA, P).T,
        lru_w=blocks.reshape(T_XA, P, 2 * P), lru_par=par,
        conv_s=a["state_conv"].reshape(NB, CW - 1, T_XA, P).transpose(2, 3, 0, 1).reshape(T_XA, P, -1),
        s5_par=np.stack([states(a["ssm_lambda_re"]), states(a["ssm_lambda_im"]),
                         states(np.broadcast_to(a["ssm_log_dt"][:, None], (G, NST)))], 1),
        s5_bc=np.stack([np.stack([states(a["ssm_b_re"]), states(a["ssm_b_im"])], 1),
                        np.stack([states(a["ssm_c_re"].transpose(0, 2, 1)), states(a["ssm_c_im"].transpose(0, 2, 1))], 1)], 1),
        s5_d=a["ssm_d"].T,
        s0=np.stack([states(a[k].transpose(1, 2, 0)) for k in ("state_ssm_re", "state_ssm_im")], 1),
        k_cache=kc.reshape(NB, P, -1), v_cache=vc.reshape(NB, P, -1),
        bias=_log_count(T - P + np.arange(P)[:, None] - np.arange(T)[None, :]),
        sbias=sbias.reshape(NB, HQ, NK),
    )
    outs = dict(y=(P, KD, N), keep=(T_KEEP, P, N), ya=(T_XA, P, N), p_ssm=(P, 2, J), s_ssm=(P, 2, J, NB))
    scratch = dict(u_d=(S5W, N), gate_d=(T_GATE, P, N), y5_d=(S5W, N), yc=(HP, P, N), x2_d=(P, KD, N))
    nc = bacc.Bacc("TRN2", target_bir_lowering=False, num_devices=1)
    feed, t = {}, {}
    for name, x in arrays.items():
        feed["in_" + name] = np.ascontiguousarray(x)
        t[name] = nc.dram_tensor("in_" + name, x.shape, F32, kind="ExternalInput").ap()
    for name, shape in outs.items():
        t[name] = nc.dram_tensor("out_" + name, shape, F32, kind="ExternalOutput").ap()
    for name, shape in scratch.items():
        t[name] = nc.dram_tensor("tmp_" + name, shape, F32, kind="Internal").ap()
    hybrid_layer(nc, t)
    got = run_bass_kernel_spmd(nc, [feed], core_ids=[0]).results[0]
    y, keep, ya, p_ssm, s_ssm = (np.asarray(got["out_" + k]) for k in outs)
    y = y.transpose(2, 1, 0).reshape(N, D)

    def kept(row, tiles, cols):
        return np.moveaxis(keep[row:row + tiles, :, cols], 2, 0).reshape(-1, tiles * P)

    def unstate(x):
        x = x.reshape((2, NST, J) + x.shape[2:])
        x = np.moveaxis(x, 2, 0).reshape((G, NST) + x.shape[3:])
        return np.moveaxis(x, (0, 1), (-2, -1)).reshape((1, -1, G, NST))

    old_new, new = slice(0, T), slice(T, N)
    xs = kept(R_XA, T_XA, new).reshape(NB, TS, LRU)
    return (y[:T].reshape(1, T, D), y[T:].reshape(NB, TS, D),
            kept(R_XA, T_XA, slice(T - CW + 1, T)).reshape(1, 1, CW - 1, LRU),
            ya[:, :, T - 1].reshape(1, 1, LRU),
            unstate(p_ssm[:, 0]), unstate(p_ssm[:, 1]),
            kept(R_K, HP, old_new).reshape(1, 1, T, HEADS, HD), kept(R_V, HP, old_new).reshape(1, 1, T, HEADS, HD),
            xs[:, TS - CW + 1:].reshape(1, NB, CW - 1, LRU),
            ya[:, :, T + TS - 1::TS].transpose(2, 0, 1).reshape(1, NB, LRU),
            unstate(s_ssm[:, 0]), unstate(s_ssm[:, 1]),
            kept(R_K, HP, new).reshape(1, NB, TS, HEADS, HD), kept(R_V, HP, new).reshape(1, NB, TS, HEADS, HD))
```

```python
from contextlib import ExitStack

import numpy as np

import concourse.bass as bass
from concourse import mybir

F32 = mybir.dt.float32
F32R = mybir.dt.float32r
ALU = mybir.AluOpType
ACT = mybir.ActivationFunctionType

P = 128
D = 1024
KD = D // P
T = 1024
NB, TS = 8, 4
NS = NB * TS
N = T + NS
NBLK, BLK = 3, (T + NS) // 3
LRU, S5W, AW, DFF = 768, 512, 768, 4096
HEADS, HD = 12, 64
HP = HEADS // 2
CW = 4
G, GC, NST = 32, 16, 64
J = G // 2
L = 8
C = T // L
EPS = 1e-6
W_MAX = 2048
GROUPS = ((128, 1), (512, 4), (2048, 16))
NEAR = 512
NCK = NEAR + (W_MAX - NEAR) // 16 * TS
KT = NCK // P
NK = NCK + NS
HQ = HEADS * TS
MASKED = -1e30
TINY = 2.0 ** -100
SCALE = HD ** -0.5

T_U, T_XA, T_Q, T_K, T_V = S5W // P, LRU // P, HP, HP, HP
T_GATE = 3 * KD
T_IN = T_U + T_XA + T_Q + T_K + T_V + T_GATE
K_B = S5W // P
K_A = K_C = LRU // P
FCH = 4
NCH = DFF // P // FCH
SINGLE, DOUBLE = 1, 2
PAIRS = ([SINGLE] * (T_IN // 2) + [DOUBLE] * 2 + [DOUBLE] * 2 + [SINGLE] * 4 + [SINGLE] * 4 + [SINGLE] * 4
         + [SINGLE] * 2 + [SINGLE, SINGLE, DOUBLE, DOUBLE] * (NCH - 1) + [DOUBLE] * 2)
P_GLU = T_IN // 2
P_B = P_GLU + 2
P_A = P_B + 2
P_C = P_A + 4
P_OUT = P_C + 4
P_MLP = P_OUT + 4
USES = [sum(PAIRS[:i]) for i in range(len(PAIRS) + 1)]
R_XA, R_Q, R_K, R_V = 0, T_XA, T_XA + T_Q, T_XA + T_Q + T_K
T_KEEP = T_XA + T_Q + T_K + T_V
TWO_PI_HI = 6.28125
TWO_PI_MID = float(np.float32(np.floor((2 * np.pi - TWO_PI_HI) * 2 ** 20) / 2 ** 20))
TWO_PI_LO = float(2 * np.pi - TWO_PI_HI - TWO_PI_MID)
ROUND = 1.5 * 2.0 ** 23


UNITS = 4 * KD
V_GRAN, P_GRAN, GRAN = {}, {}, 0
for _x in range(-1, UNITS + 1):
    if (_x + 1) % (2 * KD) == 0 and _x + 1 < UNITS:
        V_GRAN[_x + 1] = [GRAN, GRAN + 1]
        GRAN += 2
    if 0 <= _x < UNITS:
        P_GRAN[_x] = [GRAN + _k for _k in range((_x % KD) // 4 + 1)]
        GRAN += len(P_GRAN[_x])


def transposed(u):
    return P_GRAN[u][-1] + 1 if u >= 0 else P_GRAN[u + UNITS][-1] + 1 - GRAN


def wait(eng, sem, value):
    if isinstance(value, int) and value <= 0:
        return
    eng.wait_ge(sem, value)


class Steps:

    def __init__(self, eng, sem):
        self.eng, self.sem, self.n, self.base = eng, sem, 0, 0

    def __call__(self, ins):
        ins.then_inc(self.sem, 1)
        self.n += 1
        self.eng.wait_ge(self.sem, self.n + self.base)

    def repeat(self, count, body):
        n0 = self.n
        body(0)
        per = self.n - n0
        if count > 1:
            with self.eng.Fori(1, count) as i:
                self.base = (i - 1) * per if per else 0
                body(i)
                assert self.n - n0 == 2 * per
            self.base = 0
        self.n = n0 + count * per


def hybrid_layer(nc, t):
    v, s, pe = nc.vector, nc.scalar, nc.tensor
    with ExitStack() as ctx:
        def sem(name):
            return ctx.enter_context(nc.semaphore(name))

        def sems(name, n):
            return [sem(f"{name}{i}") for i in range(n)]

        def own(name, shape, dt=F32):
            return ctx.enter_context(nc.sbuf_tensor(name, shape, dt))

        w_raw = own("w_raw", [P, 2, KD * P])
        w_hi = own("w_hi", [P, 2, KD, P], F32R)
        w_lo = own("w_lo", [P, 2, KD, P], F32R)
        zeros = own("zeros", [P, KD * P])
        stage = own("stage", [P, 2, N])
        ident = own("ident", [P, P])
        ones = own("ones", [P, P])
        gains = own("gains", [P, 4, KD])
        glu_b = own("glu_b", [P, 2, K_B])
        lam = own("lam", [P, T_XA])
        lru_k = own("lru_k", [P, T_XA])
        sp = own("sp", [P, 5, T_XA])
        ROW = 4 * N
        AREA = 2 * KD * ROW
        arena = own("arena", [P, (2 * AREA + AREA // 2) // 4])
        base = nc.sbuf_base - (2 * AREA + AREA // 2)
        areas = {"A": (base, AREA), "B": (base + AREA, AREA), "R": (base + 2 * AREA, AREA // 2)}

        def at(area, off, name, shape, dt=F32):
            start, size = areas[area]
            assert off + 4 * int(np.prod(shape[1:])) <= size, name
            return nc.alloc_sbuf_tensor_at(name, shape, dt, offset=start + off)

        op_hi = at("A", 0, "op_hi", [P, KD, N], F32R)
        op_lo = at("A", AREA // 2, "op_lo", [P, KD, N], F32R)
        hid_hi = at("B", 0, "hid_hi", [P, 2 * FCH, N], F32R)
        hid_lo = at("B", AREA // 2, "hid_lo", [P, 2 * FCH, N], F32R)
        acc = at("R", 0, "acc", [P, KD, N])
        resid = at("B", 0, "resid", [P, KD, N])
        n_sq = at("B", AREA // 2, "n_sq", [P, 2, N])
        n_sum = at("B", AREA // 2 + 2 * ROW, "n_sum", [P, N])
        n_rs = at("B", AREA // 2 + 3 * ROW, "n_rs", [P, N])
        n_rstd = at("B", AREA // 2 + 4 * ROW, "n_rstd", [P, N])
        n_tmp = at("B", AREA // 2 + 5 * ROW, "n_tmp", [P, 2, N])
        gate_t = at("B", 6 * ROW, "gate_t", [P, 2, N])
        prod_t = at("B", AREA // 2 + 6 * ROW, "prod_t", [P, 2, N])

        rx = at("B", 0, "rx", [P, 2, J, L + 1, GC])
        wt = at("B", 18432, "wt", [P, 2, J, L, GC])
        z5 = at("B", 18432, "z5", [P, 2, J, C])
        ph = at("B", 34816, "ph", [P, 2, J, C])
        t5 = at("B", 51200, "t5", [P, 2, J * C])
        dec = at("R", 0, "dec", [P, J, C])
        st = at("R", 8192, "st", [P, 2, J, C + 1])
        pw = at("R", 24704, "pw", [P, 2, J, L + 1])
        pwr = at("R", 25856, "pwr", [P, 2, J, L])
        bb = at("R", 26880, "bb", [P, 2, J, GC])
        bc_in = at("R", 28928, "bc_in", [P, 2, 2, J, GC])
        s5_in = at("R", 33024, "s5_in", [P, 3, J])
        s5_d = at("R", 33216, "s5_d", [GC, G])
        s5_t = own("s5_t", [P, 24, J])
        p_fin = own("p_fin", [P, 2, J])
        wtt = at("A", 0, "wtt", [P, 2, J, P])
        toep = at("A", 16384, "toep", [P, G, P])
        kpad = at("A", 32768, "kpad", [GC, G, 7 * GC + P])
        ug = at("A", 32768, "ug", [P, G, C])
        yg = at("A", 49152, "yg", [P, G, C])
        flat = stage[:, :, :].rearrange("p b n -> p (b n)")
        us = flat[:, 0:512].rearrange("p (a g b) -> p a g b", a=2, g=G)
        ys = flat[:, 512:768].rearrange("p (g b) -> p g b", g=G)
        s0 = flat[:, 768:1024].rearrange("p (a j b) -> p a j b", a=2, j=J)
        sf = flat[:, 1024:1280].rearrange("p (a j b) -> p a j b", a=2, j=J)
        sq = flat[:, 1280:1792].rearrange("p (a j b) -> p a j b", a=4, j=J)

        def row(k):
            return at("B", k * ROW, f"lru_row{k}", [P, N])
        lru = dict(zip(("xc", "r", "i", "t", "q", "a", "u", "m", "b", "h"), (row(k) for k in range(10))))
        lru["k"] = at("B", 10 * ROW, "lru_k1", [P, 1])
        lru["h0"] = at("B", 10 * ROW + 32, "lru_h0", [P, NB])
        lru_ld = []
        for n in range(2):
            off = 10 * ROW + 64 + n * 5568
            lru_ld.append(dict(x=at("B", off, f"lru_x{n}", [P, CW - 1 + T]),
                               xs=at("B", off + 4128, f"lru_xs{n}", [P, NB, CW - 1 + TS]),
                               w=at("B", off + 4352 + 64, f"lru_w{n}", [P, 2, P]),
                               par=at("B", off + 4352 + 64 + 1024, f"lru_par{n}", [P, 16])))

        qkv = at("A", 0, "qkv", [P, 2, 3, T])
        vn = at("A", 24576, "vn", [P, 2, KD, P])
        bias = at("A", 32768, "bias", [P, T])
        sm = at("A", 36864, "sm", [P, 2, T])
        pm = at("A", 45056, "pm", [P, 2, T])
        pt = at("A", 53248, "pt", [P, 2, KD, P])
        mx = at("A", 61440, "mx", [P, 2, 4])
        yo = at("R", 0, "yo", [P, 2, T])

        kc = [at("A", 21504 * n, f"kc{n}", [P, HP, NCK]) for n in range(2)]
        vc = at("A", 43008, "vc", [P, KT, AW])
        sqd = at("R", 0, "sqd", [P, HP, NB, HQ])
        sq1 = at("R", 9216, "sq1", [P, 2, HP, HQ])
        qkvs = at("R", 11520, "qkvs", [P, 3, HP, NS])
        vnew = at("R", 13824, "vnew", [NS, HP, P])
        pts = at("R", 16896, "pts", [P, KT + 1, HQ])
        yos = at("R", 18432, "yos", [P, HP, NB, TS])
        sbias = at("R", 19200, "sbias", [HQ, NK])
        nbias = at("R", 22912, "nbias", [HQ, NB, NS])
        omask = at("R", 23936, "omask", [HQ, AW])
        osel = at("R", 27008, "osel", [HQ, AW])
        tsel = at("R", 30080, "tsel", [HQ, TS])
        mxs = at("R", 30112, "mxs", [HQ, 4])
        sms = flat[0:HQ, 0:NK]
        pms = flat[0:HQ, NK:2 * NK]

        ps = ctx.enter_context(nc.psum_tensor("ps", [P, 8, 512], F32))

        def blocks(ap):
            return ap.rearrange("p (b n) -> p b n", b=NBLK)

        def pset(b):
            return ps[:, 3 * b:3 * b + 3, 0:BLK]

        w_loaded = sems("w_loaded", 2)
        w_split = sems("w_split", 2)
        w_zero, w_half = sem("w_zero"), sem("w_half")
        mm_ready = sems("mm_ready", 2)
        mm_free = sems("mm_free", 2)
        act_own, dve_own = sem("act_own"), sem("dve_own")
        stored = sems("stored", 2)
        const_in, x_in, s5_par_in = sem("const_in"), sem("x_in"), sem("s5_par_in")

        class NormSems:
            def __init__(self, name):
                self.sq = sem(name + "_sq")
                self.added = sem(name + "_added")
                self.sum = sem(name + "_sum")
                self.rs = sem(name + "_rs")
                self.h = sem(name + "_h")
                self.hi = sem(name + "_hi")
                self.lo = sem(name + "_lo")

        n_in, n_mix, n_pre, n_ff = (NormSems(x) for x in ("n_in", "n_mix", "n_pre", "n_ff"))
        a5, d5, d5p = sem("a5"), sem("d5"), sem("d5p")
        p5 = sem("p5")
        toep_in, ug_in, us_in, yd_out, st_out = (sem(x) for x in ("toep_in", "ug_in", "us_in", "yd_out", "st_out"))
        s0_in = sem("s0_in")
        lru_in = sems("lru_in", 2)
        lru_stored = sem("lru_stored")
        lru_xc, lru_mm, lru_sig, lru_u, lru_sq, lru_h = (
            sem("lru_" + x) for x in ("xc", "mm", "sig", "u", "sq", "h"))
        lam_e, lam_a = sem("lam_e"), sem("lam_a")
        at_in = sems("at_in", 2)
        bias_in = sem("bias_in")
        at_s, at_masked, at_nb, at_p, at_pn, at_t, at_pt, at_pv, at_o = (
            sem("at_" + x) for x in ("s", "masked", "nb", "p", "pn", "t", "pt", "pv", "o"))
        yo_out = sems("yo_out", 2)
        qkvs_in = sem("qkvs_in")
        k_in, v_in = sems("k_in", 2), sem("v_in")
        sa_vt, sa_vn, sa_q1, sa_s, sa_masked, sa_nb, sa_p, sa_pn, sa_t, sa_pt, sa_pv, sa_om, sa_sel, sa_o = (
            sem("sa_" + x) for x in ("vt", "vn", "q1", "s", "masked", "nb", "p", "pn", "t", "pt", "pv", "om", "sel", "o"))
        yos_out = sem("yos_out")
        op_in = sems("op_in", 2)
        g_act, op_h, op_l = sem("g_act"), sem("op_h"), sem("op_l")
        glu_y = sem("glu_y")
        glu_h, glu_l = sem("glu_h"), sem("glu_l")
        gate_in = sems("gate_in", 2)
        merged = sem("merged")
        o_hi, o_lo = sem("o_hi"), sem("o_lo")
        x_again, x2_done, x2_out, x2_in, y_done, y_out = (
            sem(x) for x in ("x_again", "x2_done", "x2_out", "x2_in", "y_done", "y_out"))
        go = sem("go")
        sq_done, hid_h, hid_l = sem("sq_done"), sem("hid_h"), sem("hid_l")

        block = ctx.enter_context(nc.Block())

        @block.sync
        def _(sy):
            def weights(i):
                for b in range(2):
                    wait(sy, w_split[b], i)
                    src = t["w"].rearrange("(i b) p k -> i b p k", b=2)
                    src = src[i, b] if isinstance(i, int) else src[bass.ds(i, 1), b].rearrange("a p k -> p (a k)")
                    sy.dma_start(w_raw[:, b], src).then_inc(w_loaded[b], 16)

            def weight_pairs(first, last):
                with sy.Fori(first, last) as i:
                    weights(i)

            for k in range(KD):
                sy.dma_start(acc[:, k], t["x"][:, k]).then_inc(x_in, 16)
            sy.dma_start(ident[:], t["ident"]).then_inc(const_in, 16)
            sy.dma_start(ones[:], t["ones"]).then_inc(const_in, 16)
            sy.dma_start(gains[:], t["gains"]).then_inc(const_in, 16)
            sy.dma_start(glu_b[:], t["glu_b"]).then_inc(const_in, 16)
            sy.dma_start(lam[:], t["lam"]).then_inc(const_in, 16)
            weights(0)
            sy.wait_ge(n_in.h, KD)
            sy.dma_start(s5_in[:], t["s5_par"]).then_inc(s5_par_in, 16)
            sy.dma_start(bc_in[:], t["s5_bc"]).then_inc(s5_par_in, 16)
            sy.dma_start(s5_d[:], t["s5_d"]).then_inc(s5_par_in, 16)
            weight_pairs(1, P_GLU + 1)

            sy.wait_ge(d5, 3)
            for tau in range(L):
                off = (L - 1 - tau) * GC
                sy.dma_start(toep[tau * GC:(tau + 1) * GC], kpad[:, :, off:off + P]).then_inc(toep_in, 16)
            for b in range(2):
                sy.wait_ge(stored[b], 16 * (T_IN // 2))
            sy.wait_ge(d5, 4)
            sy.dma_start(s0, t["s0"]).then_inc(s0_in, 16)
            u_d = t["u_d"].rearrange("(g c) n -> c g n", c=GC)
            for a in range(2):
                for tau in range(TS):
                    row = (a * TS + tau) * GC
                    sy.dma_start(us[row:row + GC, a], u_d[:, :, T + tau * NB:T + (tau + 1) * NB]).then_inc(us_in, 16)
            sy.wait_ge(toep_in, 16 * L)
            for tau in range(L):
                sy.dma_start(ug[tau * GC:(tau + 1) * GC], u_d[:, :, tau * C:(tau + 1) * C]).then_inc(ug_in, 16)
            sy.wait_ge(d5, 8)
            sy.dma_start(t["p_ssm"], p_fin[:]).then_inc(st_out, 16)
            sy.dma_start(t["s_ssm"], sf).then_inc(st_out, 16)
            sy.wait_ge(st_out, 32)
            sy.wait_ge(p5, 5)

            def picked(x, i, b):
                x = x.rearrange("(i b) p k -> i b p k", b=2)
                return x[i, b] if isinstance(i, int) else x[bass.ds(i, 1), b].rearrange("a p k -> p (a k)")

            for n, row in enumerate((R_Q, R_K, R_V)):
                sy.dma_start(qkvs[:, n], t["keep"][row:row + HP, :, T:N].rearrange("h p n -> p h n")).then_inc(qkvs_in, 16)
            for dst, name in ((sbias[:, 0:NCK], "sbias"), (nbias[:], "nbias"), (omask[:], "omask"), (tsel[:], "tsel")):
                sy.dma_start(dst, t[name]).then_inc(qkvs_in, 16)

            def k_load(i, b):
                sy.dma_start(kc[b][:].rearrange("p h n -> p (h n)"), picked(t["k_cache"], i, b)).then_inc(k_in[b], 16)

            def v_load(i, b):
                sy.dma_start(vc[:].rearrange("p h n -> p (h n)"), picked(t["v_cache"], i, b)).then_inc(v_in, 16)

            k_load(0, 0)
            k_load(0, 1)
            sy.wait_ge(d5, 9)
            sy.wait_ge(a5, 7)
            y_d = t["y5_d"].rearrange("(g c) n -> c g n", c=GC)
            for tau in range(L):
                rows = slice(tau * GC, (tau + 1) * GC)
                sy.dma_start(y_d[:, :, tau * C:(tau + 1) * C], yg[rows]).then_inc(yd_out, 16)
                if tau < TS:
                    sy.dma_start(y_d[:, :, T + tau * NB:T + (tau + 1) * NB], ys[rows]).then_inc(yd_out, 16)
            sy.wait_ge(yd_out, 16 * (L + TS))
            v_load(0, 0)

            def sample_loads(i, b, k_too=True):
                n = 2 * i + b
                if k_too:
                    wait(sy, sa_s, n + 1)
                    k_load(i + 1, b)
                wait(sy, sa_pv, n + 1)
                v_load(i if b == 0 else i + 1, 1 - b)

            def lru_store(i, b):
                wait(sy, lru_h, 2 * i + b + 1)
                sy.dma_start(picked(t["ya"], i, b), lru["h"][:]).then_inc(lru_stored, 16)

            def round(i):
                for b in range(2):
                    sample_loads(i, b)
                    lru_store(i, b)

            round(0)
            with sy.Fori(1, T_XA // 2) as i:
                round(i)
            sample_loads(NB // 2 - 1, 0, False)
            sy.wait_ge(sa_o, NB)
            sy.dma_start(t["yc"][:, :, T:N].rearrange("h p n -> p h n"), yos[:].rearrange("p h b t -> p h (b t)")).then_inc(yos_out, 16)
            sy.wait_ge(yos_out, 16)
            sy.wait_ge(lru_stored, 16 * T_XA)

            def kept(row, i, b):
                x = t["keep"][row:row + HP].rearrange("(i b) p k -> i b p k", b=2)
                return x[i, b] if isinstance(i, int) else x[bass.ds(i, 1), b].rearrange("a p k -> p (a k)")

            def at_load(i):
                for b in range(2):
                    wait(sy, at_pv, 32 * i + 16 * b - 16)
                    for n, row in enumerate((R_Q, R_K, R_V)):
                        sy.dma_start(qkv[:, b, n], kept(row, i, b)[:, 0:T]).then_inc(at_in[b], 16)

            def at_store(i):
                for b in range(2):
                    out = t["yc"].rearrange("(i b) p k -> i b p k", b=2)
                    out = out[i, b] if isinstance(i, int) else out[bass.ds(i, 1), b].rearrange("a p k -> p (a k)")
                    wait(sy, at_o, 8 * i + 4 * b + 4)
                    sy.sem_inc(go, 1)
                    sy.dma_start(out[:, 0:T], yo[:, b]).then_inc(yo_out[b], 16)

            sy.dma_start(bias[:], t["bias"]).then_inc(bias_in, 16)
            at_load(0)
            at_store(0)
            with sy.Fori(1, HP // 2) as i:
                at_load(i)
                at_store(i)
            for b in range(2):
                sy.wait_ge(yo_out[b], 16 * (HP // 2))

            ops = [t["y5_d"].rearrange("(k p) n -> k p n", p=P)[k] for k in range(K_B)]
            for n in range(K_B):
                wait(sy, op_l, n - 1)
                sy.dma_start(stage[:, n % 2], ops[n]).then_inc(op_in[n % 2], 16)
            weights(P_GLU + 1)
            gates = t["gate_d"].rearrange("(j i b) p k -> j i b p k", j=3, b=2)

            def gate_load(branch, i, tile0):
                for b in range(2):
                    g = gates[branch]
                    g = g[i, b] if isinstance(i, int) else g[bass.ds(i, 1), b].rearrange("a p k -> p (a k)")
                    wait(sy, merged, tile0 + 2 * i + b - 1)
                    sy.dma_start(gate_t[:, b], g).then_inc(gate_in[b], 16)

            def operand_load(first, src, k):
                wait(sy, op_l, first + k - 1)
                sy.dma_start(stage[:, k % 2], src[k]).then_inc(op_in[k % 2], 16)

            gate_load(1, 0, 0)
            weights(P_B)
            for k in range(K_A):
                operand_load(K_B, t["ya"], k)
            weights(P_B + 1)
            for m in range(1, KD // 2):
                gate_load(1, m, 0)
            weights(P_A)
            gate_load(0, 0, KD)
            for k in range(K_C):
                operand_load(K_B + K_A, t["yc"], k)
            with sy.Fori(1, KD // 2) as i:
                weights(i + P_A)
                gate_load(0, i, KD)
            weights(P_C)
            gate_load(2, 0, 2 * KD)
            with sy.Fori(1, KD // 2) as i:
                weights(i + P_C)
                gate_load(2, i, 2 * KD)
            sy.wait_ge(merged, 3 * KD)
            for k in range(KD):
                sy.dma_start(resid[:, k], t["x"][:, k]).then_inc(x_again, 16)
            weight_pairs(P_OUT, P_MLP + 1)
            for k in range(KD):
                sy.wait_ge(x2_done, k + 1)
                sy.dma_start(t["x2_d"][:, k], resid[:, k]).then_inc(x2_out, 16)
            weight_pairs(P_MLP + 1, len(PAIRS))
            sy.wait_ge(x2_out, 16 * KD)
            sy.wait_ge(mm_ready[1], USES[-1])
            sy.wait_ge(mm_ready[0], USES[-1])
            for k in range(KD):
                sy.dma_start(resid[:, k], t["x2_d"][:, k]).then_inc(x2_in, 16)
            for k in range(KD):
                sy.wait_ge(y_done, k + 1)
                sy.dma_start(t["y"][:, k], resid[:, k]).then_inc(y_out, 16)
            sy.wait_ge(y_out, 16 * KD)

        @block.gpsimd
        def _(pool):
            pool.memset(zeros[:], 0.0).then_inc(w_zero, 1)
            pool.wait_ge(w_zero, 1)

            def split(i, b, used):
                if used:
                    pool.wait_ge(mm_ready[used[0]], used[1])
                pool.wait_ge(w_loaded[b], 16 * (i + 1))
                hi, lo = (w[:, b].rearrange("p k m -> p (k m)") for w in (w_hi, w_lo))
                pool.tensor_tensor(hi, w_raw[:, b], zeros[:], ALU.add).then_inc(w_half, 1)
                pool.wait_ge(w_half, 2 * i + b + 1)
                pool.tensor_tensor(lo, w_raw[:, b], hi.bitcast(F32), ALU.subtract).then_inc(w_split[b], 1)

            def pair(i, before, uses):
                for b in range(2):
                    split(i, b, (b, uses + 1) if before == SINGLE else (1, uses + 1 + b))

            def run(first, last):
                kind, u0 = PAIRS[first - 1], USES[first - 1]
                assert all(k == kind for k in PAIRS[first - 1:last - 1])
                if last - first == 1:
                    pair(first, kind, u0)
                else:
                    with pool.Fori(first, last) as i:
                        pair(i, kind, (i - first) * kind + u0)

            for b in range(2):
                split(0, b, None)
            run(1, P_GLU + 1)

            pool.wait_ge(d5, 8)

            def lru_load(i):
                for b in range(2):
                    def pick(x, i=i, b=b):
                        x = x.rearrange("(i b) p k -> i b p k", b=2)
                        return x[i, b] if isinstance(i, int) else x[bass.ds(i, 1), b].rearrange("a p k -> p (a k)")
                    z = lru_ld[b]
                    wait(pool, lru_h, 2 * i + b - 1)
                    xa = pick(t["keep"][R_XA:R_XA + T_XA])
                    for dst, src in ((z["x"][:, CW - 1:], xa[:, 0:T]),
                                     (z["xs"][:, :, CW - 1:], xa[:, T:N].rearrange("p (b t) -> p b t", b=NB)),
                                     (z["xs"][:, :, 0:CW - 1], pick(t["conv_s"]).rearrange("p (b t) -> p b t", b=NB)),
                                     (z["w"][:].rearrange("p a m -> p (a m)"), pick(t["lru_w"])),
                                     (z["par"][:], pick(t["lru_par"]))):
                        pool.dma_start(dst, src).then_inc(lru_in[b], 16)

            lru_load(0)
            with pool.Fori(1, T_XA // 2) as i:
                lru_load(i)
            run(P_GLU + 1, P_A + 1)
            run(P_A + 1, P_MLP + 3)
            first, per = P_MLP + 3, USES[P_MLP + 6] - USES[P_MLP + 2]
            with pool.Fori(0, NCH - 1) as c:
                for n in range(4):
                    pair(c * 4 + first + n, PAIRS[first + n - 1], c * per + USES[first + n - 1])
            run(len(PAIRS) - 1, len(PAIRS))

        @block.scalar
        def _(act):
            step = Steps(act, act_own)

            def squares(n, src, ready):
                for k in range(KD):
                    ready(k)
                    wait(act, n.added, k - 1)
                    s.activation(n_sq[:, k % 2], src[:, k], ACT.Square).then_inc(n.sq, 1)

            def root(n):
                act.wait_ge(n.sum, 1)
                s.activation(blocks(n_rs[:]), pset(0), ACT.Sqrt, bias=EPS, scale=1.0 / D).then_inc(n.rs, 1)

            def high_parts(n):
                for k in range(KD):
                    act.wait_ge(n.h, k + 1)
                    s.activation(op_hi[:, k], n_tmp[:, k % 2], ACT.Copy).then_inc(n.hi, 1)

            act.wait_ge(lam_a, 1)
            s.activation(sp[:, 1], sp[:, 0], ACT.Exp, scale=-1.0).then_inc(lam_e, 1)
            squares(n_in, acc, lambda k: act.wait_ge(x_in, 16 * KD))
            root(n_in)
            high_parts(n_in)
            act.wait_ge(s5_par_in, 48)
            s.activation(s5_t[:, 0], s5_in[:, 2], ACT.Tanh, scale=1.0 / 16).then_inc(a5, 1)
            act.wait_ge(d5p, 1)
            s.activation(s5_t[:, 4], s5_t[:, 2], ACT.Tanh, scale=0.5).then_inc(a5, 1)
            s.activation(s5_t[:, 5], s5_t[:, 3], ACT.Sin).then_inc(a5, 1)
            s.activation(s5_t[:, 6], s5_t[:, 3], ACT.Sin, scale=0.5).then_inc(a5, 1)

            def stage_free(i, b):
                act.wait_ge(mm_ready[b], i + 1)
                wait(act, stored[b], 16 * i)

            def store(i, b, dst):
                act.wait_ge(mm_free[b], i + 1)
                act.dma_start(dst, stage[:, b]).then_inc(stored[b], 16)

            for i in range(T_U // 2):
                for b in range(2):
                    stage_free(i, b)
                    for n in range(NBLK):
                        whole = min(BLK, T - n * BLK)
                        s.activation(
                            stage[:, b, 0:T].rearrange("p (t k) -> p k t", t=L)[:, n * BLK // L:(n * BLK + whole) // L],
                            ps[:, 3 * b + n, 0:whole].rearrange("p (k t) -> p k t", t=L), ACT.Copy)
                    s.activation(stage[:, b, T:N].rearrange("p (t b) -> p b t", t=TS),
                                 ps[:, 3 * b + 2, T - 2 * BLK:BLK].rearrange("p (b t) -> p b t", t=TS),
                                 ACT.Copy).then_inc(mm_free[b], 1)
                    store(i, b, t["u_d"][(2 * i + b) * P:(2 * i + b + 1) * P])
            for first, tiles, dst, func in ((T_U // 2, T_KEEP // 2, t["keep"], ACT.Copy),
                                            ((T_U + T_KEEP) // 2, T_GATE // 2, t["gate_d"], ACT.Sigmoid)):
                dst = dst.rearrange("(i b) p k -> i b p k", b=2)
                with act.Fori(0, tiles) as i:
                    for b in range(2):
                        stage_free(i + first, b)
                        s.activation(blocks(stage[:, b]), pset(b), func).then_inc(mm_free[b], 1)
                        store(i + first, b, dst[bass.ds(i, 1), b].rearrange("a p k -> p (a k)"))

            act.wait_ge(p5, 1)
            s.activation(wtt[:, 0], ps[:, 0:4, :].rearrange("p b (j m) -> p (b j) m", m=P), ACT.Copy).then_inc(a5, 1)
            act.wait_ge(p5, 2)
            s.activation(kpad[:].rearrange("c (j a) x -> c a j x", a=2)[:, 0, :, 7 * GC:],
                         ps[0:GC, 0:4, :].rearrange("p b (j m) -> p (b j) m", m=P), ACT.Copy).then_inc(a5, 1)
            act.wait_ge(p5, 5)
            s.activation(yg[:, 0:G:2], ps[:, 0:4, :].rearrange("p b (j m) -> p (b j) m", m=P), ACT.Copy).then_inc(a5, 1)

            def lru_acts(i, b):
                z, par, n = lru, lru_ld[b]["par"], 2 * i + b
                wait(act, lru_mm, 2 * n + 1)
                wait(act, lru_h, n)
                s.activation(blocks(z["r"][:]), ps[:, 5:8, 0:BLK], ACT.Sigmoid, bias=par[:, 5:6]).then_inc(lru_sig, 1)
                act.wait_ge(lru_sig, 3 * n + 1)
                s.activation(z["t"][:], z["r"][:], ACT.Tanh, scale=z["k"][:, 0:1]).then_inc(lru_sig, 1)
                act.wait_ge(lru_mm, 2 * n + 2)
                s.activation(blocks(z["i"][:]), ps[:, 5:8, 0:BLK], ACT.Sigmoid, bias=par[:, 6:7]).then_inc(lru_sig, 1)
                wait(act, lru_u, n + 1)
                s.activation(z["m"][:], z["u"][:], ACT.Sqrt).then_inc(lru_sq, 1)

            def sample_exp(n):
                wait(act, sa_nb, n + 1)
                wait(act, sa_t, n)
                s.activation(pms, sms, ACT.Exp, bias=mxs[:, 1:2], scale=SCALE, accum_out=mxs[:, 2:3]).then_inc(sa_p, 1)

            def sample_copy(n):
                wait(act, sa_t, n + 1)
                wait(act, sa_pv, n)
                s.activation(pts[:, 0:KT].rearrange("p j m -> p (j m)"), ps[:, 2, 0:KT * HQ], ACT.Copy)
                s.activation(pts[0:NS, KT], ps[0:NS, 2, KT * HQ:(KT + 1) * HQ], ACT.Copy).then_inc(sa_pt, 1)

            act.wait_ge(sa_vt, 1)
            s.activation(vnew[:].rearrange("p h m -> p (h m)"), ps[0:NS, 3:5, 0:384], ACT.Copy).then_inc(sa_vn, 1)
            sample_exp(0)

            def both(i):
                for b in range(2):
                    sample_copy(2 * i + b)
                    lru_acts(i, b)
                    sample_exp(2 * i + b + 1)

            both(0)
            with act.Fori(1, T_XA // 2) as i:
                both(i)
            for n in range(T_XA, NB):
                sample_copy(n)
                if n + 1 < NB:
                    sample_exp(n + 1)

            def at_acts(i):
                def exps(u):
                    h, q = u // KD, u % KD
                    p2, n = u % 2, P * (q + 1)
                    wait(act, at_nb, 32 * i + u + 1)
                    wait(act, at_t, GRAN * i + transposed(u - 2))
                    s.activation(pm[:, p2, 0:n], sm[:, p2, 0:n], ACT.Exp, bias=mx[:, p2, 1:2], scale=SCALE,
                                 accum_out=mx[:, p2, 2:3]).then_inc(at_p, 1)

                def copies(u):
                    for k, g in enumerate(P_GRAN[u]):
                        n = min(P * 4, P * (u % KD + 1) - k * 4 * P)
                        wait(act, at_t, GRAN * i + g + 1)
                        wait(act, at_pv, 32 * i + u - 1)
                        s.activation(pt[:, u % 2, 4 * k:4 * k + n // P].rearrange("p j m -> p (j m)"),
                                     ps[:, 4 + g % 2, 0:n], ACT.Copy).then_inc(at_pt, 1)

                def values(u):
                    for k, g in enumerate(V_GRAN[u]):
                        wait(act, at_t, GRAN * i + g + 1)
                        wait(act, at_pv, 32 * i + u - 16)
                        s.activation(vn[:, u // 16, 4 * k:4 * k + 4].rearrange("p j m -> p (j m)"),
                                     ps[:, 4 + g % 2, :], ACT.Copy).then_inc(at_pt, 1)

                def outputs(u):
                    if u % 4 == 3:
                        h, half = u // KD, u % KD // 4
                        rows = slice(HD * (h % 2), HD * (h % 2) + HD)
                        wait(act, at_pv, 32 * i + u + 1)
                        wait(act, yo_out[h // 2], 16 * i)
                        s.activation(yo[rows, h // 2, 512 * half:512 * half + 512], ps[rows, 6 + u // 4 % 2, :],
                                     ACT.Copy).then_inc(at_o, 1)

                for x in range(-1, 33):
                    if x + 1 < 32:
                        if (x + 1) % 16 == 0:
                            values(x + 1)
                        exps(x + 1)
                    if 0 <= x < 32:
                        copies(x)
                    if x >= 1:
                        outputs(x - 1)

            at_acts(0)
            with act.Fori(1, HP // 2) as i:
                at_acts(i)

            for k in range(K_B):
                act.wait_ge(op_in[k % 2], 16 * (k // 2 + 1))
                wait(act, op_l, k)
                s.activation(prod_t[:, 0, 0:T].rearrange("p (k t) -> p t k", t=L),
                             stage[:, k % 2, 0:T].rearrange("p (t k) -> p t k", t=L), ACT.Gelu_apprx_tanh)
                s.activation(prod_t[:, 0, T:N].rearrange("p (b t) -> p t b", t=TS),
                             stage[:, k % 2, T:N].rearrange("p (t b) -> p t b", t=TS), ACT.Gelu_apprx_tanh).then_inc(g_act, 1)
                act.wait_ge(g_act, k + 1)
                s.activation(op_hi[:, k], prod_t[:, 0], ACT.Copy).then_inc(op_h, 1)
            for n in range(K_B):
                act.wait_ge(mm_ready[1], USES[P_GLU] + n + 1)
                wait(act, glu_y, n)
                s.activation(blocks(prod_t[:, 0]), pset(1), ACT.Sigmoid, bias=glu_b[:, 1, n:n + 1]).then_inc(mm_free[1], 1)
                act.wait_ge(glu_y, n + 1)
                s.activation(op_hi[:, K_B + n], prod_t[:, 1], ACT.Copy).then_inc(glu_h, 1)

            def operand(dst, first, k):
                act.wait_ge(op_in[k % 2], 16 * ((first + 1) // 2 + k // 2 + 1))
                s.activation(dst[:, k], stage[:, k % 2], ACT.Copy).then_inc(op_h, 1)

            for k in range(K_A):
                operand(hid_hi, K_B, k)
            act.wait_ge(merged, KD)
            for k in range(K_C):
                operand(op_hi, K_B + K_A, k)
            act.wait_ge(mm_ready[1], USES[P_OUT])
            act.wait_ge(mm_ready[0], USES[P_OUT])
            for k in range(KD):
                act.wait_ge(merged, 2 * KD + k + 1)
                s.activation(op_hi[:, k], acc[:, k], ACT.Copy).then_inc(o_hi, 1)
            def o_tile(k):
                b, u = k % 2, USES[P_OUT] + k // 2
                act.wait_ge(mm_ready[b], u + 1)
                act.wait_ge(o_lo, KD)
                s.activation(blocks(acc[:, k]), pset(b), ACT.Copy).then_inc(mm_free[b], 1)
                act.wait_ge(mm_free[b], u + 1)

            squares(n_mix, acc, o_tile)
            root(n_mix)
            squares(n_pre, resid, lambda k: act.wait_ge(x2_done, k + 1))
            root(n_pre)
            high_parts(n_pre)

            def hidden(tile, c, n, uses, parity):
                b = n % 2
                wait(act, mm_ready[b], uses + n // 2 + 1)
                wait(act, sq_done, tile)
                s.activation(blocks(stage[:, 0]), pset(b), ACT.Relu).then_inc(mm_free[b], 1)
                wait(act, sq_done, tile + 1)
                s.activation(hid_hi[:, FCH * parity + n], stage[:, 1], ACT.Copy).then_inc(hid_h, 1)

            act.wait_ge(x2_out, 16 * KD)
            act.wait_ge(n_pre.lo, KD)
            for n in range(FCH):
                hidden(n, 0, n, USES[P_MLP], 0)
            per = USES[P_MLP + 6] - USES[P_MLP + 2]
            with act.Fori(0, (NCH - 2) // 2) as c2:
                for c in range(2):
                    for n in range(FCH):
                        hidden(c2 * (2 * FCH) + (FCH * (c + 1) + n), None, n, c2 * (2 * per) + (c * per + USES[P_MLP + 2]),
                               (c + 1) % 2)
            for n in range(FCH):
                hidden(FCH * (NCH - 1) + n, None, n, USES[P_MLP + 2] + (NCH - 2) * per, 1)
            act.wait_ge(mm_free[0], USES[-1])
            act.wait_ge(mm_free[1], USES[-1])
            squares(n_ff, acc, lambda k: act.wait_ge(x2_in, 16 * KD))
            root(n_ff)

        @block.vector
        def _(dve):
            step = Steps(dve, dve_own)

            def tt(out, a, b, op):
                step(v.tensor_tensor(out, a, b, op))

            def ts(out, a, x, op, y=None, op2=None):
                step(v.tensor_scalar(out, a, x, y, op, op2) if op2 else v.tensor_scalar(out, a, x, None, op))

            def add_squares(n):
                for k in range(KD):
                    dve.wait_ge(n.sq, k + 1)
                    wait(dve, n.added, k)
                    if k == 0:
                        v.tensor_copy(n_sum[:], n_sq[:, 0]).then_inc(n.added, 1)
                    else:
                        v.tensor_tensor(n_sum[:], n_sum[:], n_sq[:, k % 2], ALU.add).then_inc(n.added, 1)

            def inverse_root(n):
                dve.wait_ge(n.rs, 1)
                step(v.reciprocal(n_rstd[:], n_rs[:]))

            def normed_parts(n, src, gain):
                for k in range(KD + 1):
                    if k < KD:
                        wait(dve, n.lo, k - 1)
                        v.scalar_tensor_tensor(out=n_tmp[:, k % 2], in0=src[:, k], scalar=gains[:, gain, k:k + 1],
                                               in1=n_rstd[:], op0=ALU.mult, op1=ALU.mult).then_inc(n.h, 1)
                    if k:
                        dve.wait_ge(n.hi, k)
                        v.tensor_tensor(op_lo[:, k - 1], n_tmp[:, (k - 1) % 2], op_hi[:, k - 1].bitcast(F32),
                                        ALU.subtract).then_inc(n.lo, 1)

            def add_normed(n, gain, done):
                for k in range(KD):
                    step(v.scalar_tensor_tensor(out=n_tmp[:, 0], in0=acc[:, k], scalar=gains[:, gain, k:k + 1],
                                                in1=n_rstd[:], op0=ALU.mult, op1=ALU.mult))
                    v.tensor_tensor(resid[:, k], resid[:, k], n_tmp[:, 0], ALU.add).then_inc(done, 1)
                    dve.wait_ge(done, k + 1)

            dve.wait_ge(const_in, 80)
            v.scalar_tensor_tensor(out=sp[:, 0], in0=lam[:], scalar=-1.0, in1=lam[:], op0=ALU.mult,
                                   op1=ALU.max).then_inc(lam_a, 1)
            dve.wait_ge(lam_e, 1)
            ts(sp[:, 2], sp[:, 1], 2.0, ALU.add)
            step(v.reciprocal(sp[:, 2], sp[:, 2]))
            tt(sp[:, 1], sp[:, 1], sp[:, 2], ALU.mult)
            tt(sp[:, 2], sp[:, 1], sp[:, 1], ALU.mult)
            ts(sp[:, 3], sp[:, 2], 1.0 / 17, ALU.mult)
            for n in range(15, 1, -2):
                step(v.scalar_tensor_tensor(out=sp[:, 3], in0=sp[:, 3], scalar=1.0 / n, in1=sp[:, 2], op0=ALU.add, op1=ALU.mult))
            step(v.scalar_tensor_tensor(out=sp[:, 3], in0=sp[:, 3], scalar=1.0, in1=sp[:, 1], op0=ALU.add, op1=ALU.mult))
            ts(sp[:, 4], lam[:], -1.0, ALU.mult, 0.0, ALU.max)
            step(v.scalar_tensor_tensor(out=sp[:, 3], in0=sp[:, 3], scalar=2.0, in1=sp[:, 4], op0=ALU.mult, op1=ALU.add))
            ts(lru_k[:], sp[:, 3], -4.0, ALU.mult)

            add_squares(n_in)
            inverse_root(n_in)
            normed_parts(n_in, acc, 0)

            def tiny(k):
                return s5_t[:, k]

            def wide(x, n):
                return x.unsqueeze(2).broadcast_to([P, J, n])

            def cmul(o, a, b, t1, t2, conj=False, negate_im=False):
                tt(t1, a[0], b[0], ALU.mult)
                tt(t2, a[1], b[1], ALU.mult)
                tt(o[0], t1, t2, ALU.add if conj else ALU.subtract)
                tt(t1, a[0], b[1], ALU.mult)
                tt(t2, a[1], b[0], ALU.mult)
                if negate_im:
                    step(v.scalar_tensor_tensor(out=o[1], in0=t1, scalar=-1.0, in1=t2, op0=ALU.mult, op1=ALU.subtract))
                else:
                    tt(o[1], t1, t2, ALU.subtract if conj else ALU.add)

            def from_tanh(o, th, t1):
                ts(t1, th, -1.0, ALU.mult, 1.0, ALU.add)
                step(v.reciprocal(t1, t1))
                step(v.scalar_tensor_tensor(out=o, in0=th, scalar=1.0, in1=t1, op0=ALU.add, op1=ALU.mult))

            def unit(re, im, t1, t2):
                tt(t1, re, re, ALU.mult)
                tt(t2, im, im, ALU.mult)
                tt(t1, t1, t2, ALU.add)
                ts(t1, t1, -0.5, ALU.mult, 1.5, ALU.add)
                tt(re, re, t1, ALU.mult)
                tt(im, im, t1, ALU.mult)

            lr, li = s5_in[:, 0], s5_in[:, 1]
            dve.wait_ge(s5_par_in, 48)
            dve.wait_ge(a5, 1)
            from_tanh(tiny(1), tiny(0), tiny(20))
            for _ in range(3):
                tt(tiny(1), tiny(1), tiny(1), ALU.mult)
            tt(tiny(2), lr, tiny(1), ALU.mult)
            tt(tiny(7), li, tiny(1), ALU.mult)
            ts(tiny(8), tiny(7), 1.0 / (2 * np.pi), ALU.mult)
            ts(tiny(8), tiny(8), ROUND, ALU.add)
            ts(tiny(8), tiny(8), ROUND, ALU.subtract)
            for part in (TWO_PI_HI, TWO_PI_MID, TWO_PI_LO):
                step(v.scalar_tensor_tensor(out=tiny(7), in0=tiny(8), scalar=-part, in1=tiny(7), op0=ALU.mult, op1=ALU.add))
            v.tensor_scalar(tiny(3), tiny(7), 3.1415925, -3.1415925, ALU.min, ALU.max).then_inc(d5p, 1)
            dve.wait_ge(a5, 4)
            dve.wait_ge(d5p, 1)
            from_tanh(tiny(9), tiny(4), tiny(20))
            tt(tiny(10), tiny(6), tiny(6), ALU.mult)
            ts(tiny(10), tiny(10), -2.0, ALU.mult, 1.0, ALU.add)
            step(v.tensor_copy(tiny(11), tiny(5)))
            unit(tiny(10), tiny(11), tiny(20), tiny(21))
            step(v.memset(pw[:, 0, :, 0:1], 1.0))
            step(v.memset(pw[:, 1, :, 0:1], 0.0))
            for k in range(2):
                tt(pw[:, k, :, 1], tiny(9), tiny(10 + k), ALU.mult)
            t1, t2 = (t5[:, k, :].rearrange("p (j k) -> p j k", j=J) for k in range(2))
            for n in (1, 2, 4):
                cmul([pw[:, k, :, n + 1:2 * n + 1] for k in range(2)], [pw[:, k, :, 1:n + 1] for k in range(2)],
                     [wide(pw[:, k, :, n], n) for k in range(2)], t1[:, :, 0:n], t2[:, :, 0:n])
            for n in range(L):
                step(v.tensor_copy(pwr[:, :, :, n], pw[:, :, :, L - 1 - n]))
            step(v.tensor_copy(tiny(12), tiny(9)))
            for _ in range(3):
                tt(tiny(12), tiny(12), tiny(12), ALU.mult)
            step(v.tensor_copy(dec[:], wide(tiny(12), C)))
            step(v.memset(dec[:, :, 0:1], 0.0))
            m, m2 = [tiny(10), tiny(11)], [tiny(13), tiny(14)]
            for _ in range(3):
                cmul(m2, m, m, tiny(20), tiny(21))
                m, m2 = m2, m
            unit(m[0], m[1], tiny(20), tiny(21))
            step(v.memset(ph[:, 0, :, 0:1], 1.0))
            step(v.memset(ph[:, 1, :, 0:1], 0.0))
            n = 1
            while n < C:
                cmul([ph[:, k, :, n:2 * n] for k in range(2)], [ph[:, k, :, 0:n] for k in range(2)],
                     [wide(m[k], n) for k in range(2)], t1[:, :, 0:n], t2[:, :, 0:n])
                n *= 2
                if n < C:
                    cmul(m2, m, m, tiny(20), tiny(21))
                    m, m2 = m2, m
                    unit(m[0], m[1], tiny(20), tiny(21))
            ts(tiny(15), pw[:, 0, :, 1], -1.0, ALU.add)
            ai = pw[:, 1, :, 1]
            tt(tiny(16), tiny(15), lr, ALU.mult)
            tt(tiny(17), ai, li, ALU.mult)
            tt(tiny(16), tiny(16), tiny(17), ALU.add)
            tt(tiny(17), ai, lr, ALU.mult)
            tt(tiny(18), tiny(15), li, ALU.mult)
            tt(tiny(17), tiny(17), tiny(18), ALU.subtract)
            tt(tiny(18), lr, lr, ALU.mult)
            tt(tiny(19), li, li, ALU.mult)
            tt(tiny(18), tiny(18), tiny(19), ALU.add)
            step(v.reciprocal(tiny(18), tiny(18)))
            tt(tiny(16), tiny(16), tiny(18), ALU.mult)
            tt(tiny(17), tiny(17), tiny(18), ALU.mult)
            cmul([bb[:, 0], bb[:, 1]], [wide(tiny(16), GC), wide(tiny(17), GC)], [bc_in[:, 0, 0], bc_in[:, 0, 1]],
                 t1[:, :, 0:GC], t2[:, :, 0:GC])
            for n in range(L):
                cmul([wt[:, 0, :, n], wt[:, 1, :, n]], [wide(pwr[:, k, :, n], GC) for k in range(2)], [bb[:, 0], bb[:, 1]],
                     t1[:, :, 0:GC], t2[:, :, 0:GC])
            for n in range(L + 1):
                cmul([rx[:, 0, :, n], rx[:, 1, :, n]], [wide(pw[:, k, :, n], GC) for k in range(2)],
                     [bc_in[:, 1, 0], bc_in[:, 1, 1]], t1[:, :, 0:GC], t2[:, :, 0:GC], negate_im=True)
            step(v.memset(st[:, :, :, 0:1], 0.0))
            v.memset(s5_t[:, 22:24], 0.0).then_inc(d5, 1)

            dve.wait_ge(p5, 1)
            v.tensor_copy(wtt[:, 1], ps[:, 4:8, :].rearrange("p b (j m) -> p (b j) m", m=P)).then_inc(d5, 1)
            step(v.memset(kpad[:, :, 0:7 * GC], 0.0))
            dve.wait_ge(p5, 2)
            step(v.tensor_copy(kpad[:].rearrange("c (j a) x -> c a j x", a=2)[:, 1, :, 7 * GC:],
                               ps[0:GC, 4:8, :].rearrange("p b (j m) -> p (b j) m", m=P)))
            diag = t5[0:GC, 0, 0:G * GC].rearrange("p (g c) -> p g c", g=G)
            tt(diag, s5_d[:].unsqueeze(2).broadcast_to([GC, G, GC]), ident[0:GC, 0:GC].unsqueeze(1).broadcast_to([GC, G, GC]), ALU.mult)
            dve.wait_ge(a5, 6)
            now = kpad[:, :, 7 * GC:8 * GC]
            v.tensor_tensor(now, now, diag, ALU.add).then_inc(d5, 1)
            for b in range(2):
                dve.wait_ge(stored[b], 16 * (T_IN // 2))
            v.memset(us, 0.0).then_inc(d5, 1)
            dve.wait_ge(p5, 3)
            vps = [ps[:, 4 * k:4 * k + 4, :].rearrange("p b (j m) -> p (b j) m", m=C) for k in range(2)]
            cmul([z5[:, 0], z5[:, 1]], [ph[:, 0], ph[:, 1]], vps, t1, t2, conj=True)
            flat_dec = dec[:].rearrange("p j k -> p (j k)")
            for k in range(2):
                ins = v.tensor_tensor_scan(out=t5[:, k], data0=flat_dec, data1=z5[:, k].rearrange("p j k -> p (j k)"),
                                           initial=0.0, op0=ALU.mult, op1=ALU.add)
                if k == 0:
                    ins.then_inc(d5, 1)
                else:
                    step(ins)
            dve.wait_ge(d5, 5)
            cmul([st[:, 0, :, 1:], st[:, 1, :, 1:]], [ph[:, 0], ph[:, 1]], [t1, t2], z5[:, 0], z5[:, 1])
            step(v.tensor_copy(p_fin[:], st[:, :, :, C]))
            v.memset(s5_t[:, 22:24], 0.0).then_inc(d5, 1)
            dve.wait_ge(p5, 4)
            dve.wait_ge(s0_in, 16)
            vs = [ps[:, 0, k * J * NB:(k + 1) * J * NB].rearrange("p (j b) -> p j b", j=J) for k in range(2)]
            cmul([sq[:, 0], sq[:, 1]], [wide(pw[:, k, :, TS], NB) for k in range(2)], [s0[:, 0], s0[:, 1]],
                 sq[:, 2], sq[:, 3])
            tt(sf[:, 0], sq[:, 0], vs[0], ALU.add)
            tt(sf[:, 1], sq[:, 1], vs[1], ALU.add)
            v.tensor_copy(ys.rearrange("p (j a) b -> p j a b", a=2),
                          ps[:, 1:3, 0:J * NB].rearrange("p a (j b) -> p j a b", b=NB)).then_inc(d5, 1)
            v.memset(s5_t[:, 22:24], 0.0).then_inc(d5, 1)
            dve.wait_ge(p5, 5)
            v.tensor_copy(yg[:, 1:G:2], ps[:, 4:8, :].rearrange("p b (j m) -> p (b j) m", m=P)).then_inc(d5, 1)

            def lru_conv(i, b):
                z, n, x, xs, par = lru, 2 * i + b, lru_ld[b]["x"], lru_ld[b]["xs"], lru_ld[b]["par"]
                dve.wait_ge(lru_in[b], 80 * (i + 1))
                step(v.tensor_copy(z["k"][:], lru_k[:, bass.ds(i * 2 + b, 1)] if not isinstance(i, int) else lru_k[:, n:n + 1]))
                if isinstance(i, int):
                    step(v.memset(x[:, 0:CW - 1], 0.0))
                for k in range(CW):
                    for src, out in ((x[:, k:k + T], z["xc"][:, 0:T]),
                                     (xs[:, :, k:k + TS], z["xc"][:, T:N].rearrange("p (b t) -> p b t", b=NB))):
                        if k == 0:
                            ts(out, src, par[:, 0:1], ALU.mult, par[:, 4:5], ALU.add)
                        else:
                            step(v.scalar_tensor_tensor(out=out, in0=src, scalar=par[:, k:k + 1], in1=out,
                                                        op0=ALU.mult, op1=ALU.add))
                dve.sem_inc(lru_xc, 1)

            def lru_decay(i, b):
                z, n = lru, 2 * i + b
                dve.wait_ge(lru_sig, 3 * n + 2)
                v.tensor_scalar(z["u"][:], z["t"][:], -1.0, TINY, ALU.mult, ALU.max).then_inc(lru_u, 1)
                ts(z["r"][:], z["t"][:], -1.0, ALU.mult, 1.0, ALU.add)
                step(v.reciprocal(z["q"][:], z["r"][:]))
                ts(z["a"][:], z["q"][:], 2.0, ALU.mult, -1.0, ALU.add)

            def lru_scan(i, b):
                z, n, par = lru, 2 * i + b, lru_ld[b]["par"]
                dve.wait_ge(lru_sig, 3 * n + 3)
                tt(z["i"][:], z["i"][:], z["xc"][:], ALU.mult)
                dve.wait_ge(lru_sq, n + 1)
                step(v.scalar_tensor_tensor(out=z["b"][:], in0=z["m"][:], scalar=2.0, in1=z["q"][:], op0=ALU.mult, op1=ALU.mult))
                tt(z["b"][:], z["b"][:], z["i"][:], ALU.mult)
                a0, b0 = z["a"][:, T:N:TS], z["b"][:, T:N:TS]
                tt(z["h0"][:], a0, par[:, 8:16], ALU.mult)
                tt(b0, b0, z["h0"][:], ALU.add)
                step(v.memset(a0, 0.0))
                wait(dve, lru_stored, 16 * n)
                v.tensor_tensor_scan(out=z["h"][:], data0=z["a"][:], data1=z["b"][:], initial=0.0,
                                     op0=ALU.mult, op1=ALU.add).then_inc(lru_h, 1)
                dve.wait_ge(lru_h, n + 1)

            def sample_query(i, b):
                src = sqd[:].rearrange("p h (i b) m -> p h i b m", b=2)
                new = nbias[:].rearrange("p (i b) m -> p i b m", b=2)
                if isinstance(i, int):
                    src, new = src[:, :, i, b], new[:, i, b]
                else:
                    src = src[:, :, bass.ds(i, 1), b].rearrange("p h a m -> p h (a m)")
                    new = new[:, bass.ds(i, 1), b].rearrange("p a m -> p (a m)")
                wait(dve, sa_s, 2 * i + b - 1)
                step(v.tensor_copy(sbias[:, NCK:], new))
                v.tensor_copy(sq1[:, b], src).then_inc(sa_q1, 1)

            def sample_max(n):
                dve.wait_ge(sa_s, n + 1)
                wait(dve, sa_p, n)
                dve.sem_inc(go, 1)
                v.tensor_tensor_reduce(sms, ps[0:HQ, 0:2, :].rearrange("p b n -> p (b n)")[:, 0:NK],
                                       sbias[:], 1.0, MASKED * 2, ALU.add, ALU.max, mxs[:, 0:1]).then_inc(sa_masked, 1)
                dve.wait_ge(sa_masked, n + 1)
                v.tensor_scalar(mxs[:, 1:2], mxs[:, 0:1], -SCALE, None, ALU.mult).then_inc(sa_nb, 1)

            def sample_norm(n):
                dve.wait_ge(sa_p, n + 1)
                step(v.reciprocal(mxs[:, 3:4], mxs[:, 2:3]))
                v.tensor_scalar(pms, pms, mxs[:, 3:4], None, ALU.mult).then_inc(sa_pn, 1)

            def sample_own(n):
                dve.wait_ge(sa_pv, n + 1)
                wait(dve, sa_sel, n)
                v.tensor_tensor(osel[:].rearrange("p (b n) -> p b n", b=2), ps[0:HQ, 3:5, 0:384],
                                omask[:].rearrange("p (b n) -> p b n", b=2), ALU.mult).then_inc(sa_om, 1)

            def sample_out(i, b):
                dve.wait_ge(sa_sel, 2 * i + b + 1)
                out = yos[:].rearrange("p h (i b) t -> p h i b t", b=2)
                out = out[:, :, i, b] if isinstance(i, int) else out[:, :, bass.ds(i, 1), b].rearrange("p h a t -> p h (a t)")
                v.tensor_copy(out, ps[:, 2, 400:400 + HP * TS].rearrange("p (h t) -> p h t", t=TS)).then_inc(sa_o, 1)

            dve.wait_ge(qkvs_in, 16 * 7)
            step(v.memset(sqd[:], 0.0))
            for h in range(HEADS):
                rows = slice(HD * (h % 2), HD * (h % 2) + HD)
                step(v.tensor_copy(sqd[rows, h // 2, :, h * TS:(h + 1) * TS],
                                   qkvs[rows, 0, h // 2].rearrange("p (b t) -> p b t", b=NB)))
            sample_query(0, 0)
            dve.wait_ge(yd_out, 16 * (L + TS))
            sample_max(0)

            def both(i):
                for b in range(2):
                    n = 2 * i + b
                    sample_norm(n)
                    sample_query(i if b == 0 else i + 1, 1 - b)
                    lru_conv(i, b)
                    lru_decay(i, b)
                    sample_max(n + 1)
                    lru_scan(i, b)
                    sample_own(n)
                    sample_out(i, b)

            n0 = step.n
            both(0)
            per = step.n - n0
            with dve.Fori(1, T_XA // 2) as i:
                step.base = (i - 1) * (per - 2)
                both(i)
            step.base = 0
            step.n = n0 + per + (T_XA // 2 - 1) * (per - 2)
            for n in range(T_XA, NB):
                sample_norm(n)
                if n + 1 < NB:
                    sample_query((n + 1) // 2, (n + 1) % 2)
                if n + 1 < NB:
                    sample_max(n + 1)
                sample_own(n)
                sample_out(n // 2, n % 2)

            dve.wait_ge(bias_in, 16)

            def at_round(i):
                def maxima(u):
                    q, p2, n = u % KD, u % 2, P * (u % KD + 1)
                    dve.wait_ge(at_s, UNITS * i + u + 1)
                    wait(dve, at_p, UNITS * i + u - 1)
                    dve.sem_inc(go, 1)
                    v.tensor_tensor_reduce(sm[:, p2, 0:n], ps[:, 2 * p2:2 * p2 + 2, :].rearrange("p b n -> p (b n)")[:, 0:n],
                                           bias[:, T - n:T], 1.0, MASKED * 2, ALU.add, ALU.max,
                                           mx[:, p2, 0:1]).then_inc(at_masked, 1)
                    dve.wait_ge(at_masked, UNITS * i + u + 1)
                    v.tensor_scalar(mx[:, p2, 1:2], mx[:, p2, 0:1], -SCALE, None, ALU.mult).then_inc(at_nb, 1)

                def normed(u):
                    p2, n = u % 2, P * (u % KD + 1)
                    dve.wait_ge(at_p, UNITS * i + u + 1)
                    step(v.reciprocal(mx[:, p2, 3:4], mx[:, p2, 2:3]))
                    v.tensor_scalar(pm[:, p2, 0:n], pm[:, p2, 0:n], mx[:, p2, 3:4], None, ALU.mult).then_inc(at_pn, 1)

                for x in range(-1, UNITS):
                    if x + 1 < UNITS:
                        maxima(x + 1)
                    if x >= 0:
                        normed(x)

            step.repeat(HP // 2, at_round)

            for k in range(K_B):
                dve.wait_ge(op_h, k + 1)
                v.tensor_tensor(op_lo[:, k], prod_t[:, 0], op_hi[:, k].bitcast(F32), ALU.subtract).then_inc(op_l, 1)
            for n in range(K_B):
                dve.wait_ge(mm_ready[0], USES[P_GLU] + n + 1)
                dve.wait_ge(mm_free[1], USES[P_GLU] + n + 1)
                wait(dve, glu_l, n)
                v.scalar_tensor_tensor(out=blocks(prod_t[:, 1]), in0=pset(0), scalar=glu_b[:, 0, n:n + 1],
                                       in1=blocks(prod_t[:, 0]), op0=ALU.add, op1=ALU.mult).then_inc(glu_y, 1)
                dve.wait_ge(glu_y, n + 1)
                dve.sem_inc(mm_free[0], 1)
                dve.wait_ge(glu_h, n + 1)
                v.tensor_tensor(op_lo[:, K_B + n], prod_t[:, 1], op_hi[:, K_B + n].bitcast(F32), ALU.subtract).then_inc(glu_l, 1)
            for k in range(K_A):
                dve.wait_ge(op_h, K_B + k + 1)
                v.tensor_tensor(hid_lo[:, k], stage[:, k % 2], hid_hi[:, k].bitcast(F32), ALU.subtract).then_inc(op_l, 1)
            dve.wait_ge(glu_l, K_B)
            for n in range(KD):
                b = n % 2
                dve.wait_ge(mm_ready[b], USES[P_B] + n // 2 + 1)
                dve.wait_ge(gate_in[b], 16 * (n // 2 + 1))
                v.tensor_tensor(blocks(acc[:, n]), pset(b), blocks(gate_t[:, b]), ALU.mult).then_inc(merged, 1)
                dve.wait_ge(merged, n + 1)
                dve.sem_inc(mm_free[b], 1)

            def add_branch(first_pair, done):
                def tiles(i):
                    for b in range(2):
                        n = 2 * i + b
                        dve.wait_ge(mm_ready[b], USES[first_pair] + 1 + i)
                        dve.wait_ge(gate_in[b], 16 * (done // 2 + 1) + 16 * i)
                        v.tensor_tensor(blocks(prod_t[:, b]), pset(b), blocks(gate_t[:, b]), ALU.mult).then_inc(mm_free[b], 1)
                        dve.wait_ge(mm_free[b], USES[first_pair] + 1 + i)
                        a = acc[:].rearrange("p (i b) n -> p i b n", b=2)
                        a = a[:, i, b] if isinstance(i, int) else a[:, bass.ds(i, 1), b].rearrange("p a n -> p (a n)")
                        v.tensor_tensor(a, a, prod_t[:, b], ALU.add).then_inc(merged, 1)
                        dve.wait_ge(merged, n + (done + 1))
                step.repeat(KD // 2, tiles)

            for k in range(K_C):
                dve.wait_ge(op_h, K_B + K_A + k + 1)
                v.tensor_tensor(op_lo[:, k], stage[:, k % 2], op_hi[:, k].bitcast(F32), ALU.subtract).then_inc(op_l, 1)
            add_branch(P_A, KD)
            add_branch(P_C, 2 * KD)
            for k in range(KD):
                dve.wait_ge(o_hi, k + 1)
                v.tensor_tensor(op_lo[:, k], acc[:, k], op_hi[:, k].bitcast(F32), ALU.subtract).then_inc(o_lo, 1)

            add_squares(n_mix)
            inverse_root(n_mix)
            dve.wait_ge(x_again, 16 * KD)
            add_normed(n_mix, 1, x2_done)
            step(v.memset(acc[:], 0.0))
            add_squares(n_pre)
            inverse_root(n_pre)
            normed_parts(n_pre, resid, 2)

            def hidden(tile, n, parity):
                b = n % 2
                wait(dve, mm_free[b], tile[1] + n // 2 + 1)
                v.tensor_tensor(stage[:, 1], stage[:, 0], stage[:, 0], ALU.mult).then_inc(sq_done, 1)
                dve.wait_ge(hid_h, tile[0] + 1)
                v.tensor_tensor(hid_lo[:, FCH * parity + n], stage[:, 1], hid_hi[:, FCH * parity + n].bitcast(F32),
                                ALU.subtract).then_inc(hid_l, 1)
                dve.wait_ge(hid_l, tile[0] + 1)

            def sums(uses):
                for n in range(KD):
                    b = n % 2
                    dve.wait_ge(mm_ready[b], uses + (n // 2 + 1))
                    v.tensor_tensor(blocks(acc[:, n]), blocks(acc[:, n]), pset(b), ALU.add).then_inc(mm_free[b], 1)

            dve.wait_ge(x2_out, 16 * KD)
            dve.wait_ge(n_pre.lo, KD)
            for n in range(FCH):
                hidden((n, USES[P_MLP]), n, 0)
            per = USES[P_MLP + 6] - USES[P_MLP + 2]
            u1 = USES[P_MLP + 2]
            with dve.Fori(0, (NCH - 2) // 2) as c2:
                for c in range(2):
                    for n in range(FCH):
                        hidden((c2 * (2 * FCH) + (FCH * (c + 1) + n), c2 * (2 * per) + (c * per + u1)), n, (c + 1) % 2)
                    sums(c2 * (2 * per) + (c * per + u1 + 2))
            last = u1 + (NCH - 2) * per
            for n in range(FCH):
                hidden((FCH * (NCH - 1) + n, last), n, 1)
            sums(last + 2)
            sums(last + per)
            add_squares(n_ff)
            inverse_root(n_ff)
            dve.wait_ge(x2_in, 16 * KD)
            add_normed(n_ff, 3, y_done)

        @block.tensor
        def _(te):
            def product(i, b, kts, dst, w0, hi, lo, ready, uses):
                wait(te, w_split[b], i + 1)
                wait(te, mm_free[dst], uses)
                for n, k in enumerate(kts):
                    ready(k)
                    for part, (w, x) in enumerate(((w_hi, hi), (w_hi, lo), (w_lo, hi))):
                        for q in range(NBLK):
                            mm = pe.matmul(ps[:, 3 * dst + q, 0:BLK], w[:, b, w0 + n], x[:, k, q * BLK:(q + 1) * BLK],
                                           start=(n == 0 and part == 0), stop=(n == len(kts) - 1 and part == 2))
                mm.then_inc(mm_ready[dst], 1)

            def nothing(k):
                pass

            def sum_squares(n, uses):
                te.wait_ge(n.added, KD)
                wait(te, mm_free[0], uses)
                for q in range(NBLK):
                    mm = pe.matmul(ps[:, q, 0:BLK], ones[:], n_sum[:, q * BLK:(q + 1) * BLK], start=True, stop=True)
                mm.then_inc(n.sum, 1)

            te.wait_ge(const_in, 80)
            sum_squares(n_in, 0)
            for b in range(2):
                product(0, b, range(KD), b, 0, op_hi, op_lo, lambda k: te.wait_ge(n_in.lo, k + 1), 0)
            with te.Fori(1, T_IN // 2) as i:
                for b in range(2):
                    product(i, b, range(KD), b, 0, op_hi, op_lo, nothing, i)

            te.wait_ge(d5, 1)
            for b in range(2):
                te.wait_ge(mm_free[b], T_IN // 2)
            for a in range(2):
                for j in range(J):
                    mm = pe.transpose(ps[:, 4 * a + j // 4, P * (j % 4):P * (j % 4) + P],
                                      wt[:, a, j].rearrange("p t c -> p (t c)"), ident[:])
            mm.then_inc(p5, 1)
            te.wait_ge(a5, 5)
            te.wait_ge(d5, 2)
            for a in range(2):
                rows = slice(NST * a, NST * a + NST)
                for j in range(J):
                    for part in range(2):
                        mm = pe.matmul(ps[0:GC, 4 * a + j // 4, P * (j % 4):P * (j % 4) + P], bb[rows, part, j],
                                       rx[rows, part, j, 0:L].rearrange("p t c -> p (t c)"),
                                       start=(part == 0), stop=(part == 1))
            mm.then_inc(p5, 1)
            te.wait_ge(ug_in, 16 * L)
            te.wait_ge(a5, 6)
            te.wait_ge(d5, 3)
            for g in range(G):
                j, a = g // 2, g % 2
                for part in range(2):
                    mm = pe.matmul(ps[NST * a:NST * a + NST, 4 * part + j // 4, C * (j % 4):C * (j % 4) + C],
                                   wtt[:, part, j, NST * a:NST * a + NST], ug[:, g], start=True, stop=True)
            mm.then_inc(p5, 1)
            te.wait_ge(us_in, 16 * 2 * TS)
            te.wait_ge(s0_in, 16)
            te.wait_ge(toep_in, 16 * L)
            te.wait_ge(d5, 5)
            for g in range(G):
                j, a = g // 2, g % 2
                rows = slice(NST * a, NST * a + NST)
                for part in range(2):
                    at0 = (part * J + j) * NB
                    pe.matmul(ps[rows, 0, at0:at0 + NB], wtt[:, part, j, rows], us[:, 1, g], start=True, stop=True)
                pe.matmul(ps[:, 1 + a, j * NB:(j + 1) * NB], toep[:, g], us[:, 0, g], start=True, stop=False)
                for part in range(2):
                    mm = pe.matmul(ps[:, 1 + a, j * NB:(j + 1) * NB], rx[rows, part, j, 1:].rearrange("p t c -> p (t c)"),
                                   s0[rows, part, j], start=False, stop=(part == 1))
            mm.then_inc(p5, 1)
            te.wait_ge(d5, 8)
            for g in range(G):
                j, a = g // 2, g % 2
                rows = slice(NST * a, NST * a + NST)
                out = ps[:, 4 * a + j // 4, C * (j % 4):C * (j % 4) + C]
                pe.matmul(out, toep[:, g], ug[:, g], start=True, stop=False)
                for part in range(2):
                    mm = pe.matmul(out, rx[rows, part, j, 1:].rearrange("p t c -> p (t c)"), st[rows, part, j, 0:C],
                                   start=False, stop=(part == 1))
            mm.then_inc(p5, 1)

            te.wait_ge(a5, 7)
            te.wait_ge(d5, 9)
            te.wait_ge(qkvs_in, 16 * 7)
            for h in range(HP):
                mm = pe.transpose(ps[0:NS, 3 + h // 3, P * (h % 3):P * (h % 3) + P], qkvs[:, 2, h], ident[:])
            mm.then_inc(sa_vt, 1)

            def lru_gate(i, b, a):
                z, n = lru_ld[b], 2 * i + b
                te.wait_ge(lru_xc, n + 1)
                te.wait_ge(lru_in[b], 80 * (i + 1))
                wait(te, lru_sig, 3 * n + (1 if a else 0))
                for q in range(NBLK):
                    mm = pe.matmul(ps[:, 5 + q, 0:BLK], z["w"][:, a], lru["xc"][:, q * BLK:(q + 1) * BLK],
                                   start=True, stop=True)
                mm.then_inc(lru_mm, 1)

            def sample_scores(i, b, half):
                if half == 0:
                    te.wait_ge(k_in[b], 16 * (i + 1))
                    te.wait_ge(sa_q1, 2 * i + b + 1)
                    wait(te, sa_masked, 2 * i + b)
                for bank, lo, cols, keys in ((0, 0, 512, kc[b][:, :, 0:512]), (1, 0, NCK - 512, kc[b][:, :, 512:NCK]),
                                             (1, NCK - 512, NS, qkvs[:, 1])):
                    for h in range(HP if bank == half else 0):
                        mm = pe.matmul(ps[0:HQ, bank, lo:lo + cols], sq1[:, b, h], keys[:, h],
                                       start=(h == 0), stop=(h == HP - 1))
                if half:
                    mm.then_inc(sa_s, 1)

            def sample_transposes(n):
                te.wait_ge(sa_pn, n + 1)
                te.sem_inc(go, 1)
                for j in range(KT + 1):
                    m = P if j < KT else NS
                    mm = pe.transpose(ps[0:m, 2, HQ * j:HQ * j + HQ], pms[:, P * j:P * j + m], ident[0:HQ, 0:HQ])
                mm.then_inc(sa_t, 1)

            def sample_values(n, half):
                if half == 0:
                    te.wait_ge(v_in, 16 * (n + 1))
                    te.wait_ge(sa_pt, n + 1)
                    wait(te, sa_om, n)
                for j in range(KT + 1):
                    m = P if j < KT else NS
                    rhs = vc[:, j, 384 * half:384 * half + 384] if j < KT else \
                        vnew[:, 3 * half:3 * half + 3].rearrange("p h m -> p (h m)")
                    mm = pe.matmul(ps[0:HQ, 3 + half, 0:384], pts[0:m, j], rhs, start=(j == 0), stop=(j == KT))
                if half:
                    mm.then_inc(sa_pv, 1)

            def sample_select(n):
                te.wait_ge(sa_om, n + 1)
                wait(te, sa_o, n)
                te.sem_inc(go, 1)
                for h in range(HP):
                    mm = pe.matmul(ps[:, 2, 400 + TS * h:400 + TS * (h + 1)], osel[:, P * h:P * h + P], tsel[:],
                                   start=True, stop=True)
                mm.then_inc(sa_sel, 1)

            for half in range(2):
                sample_scores(0, 0, half)
            te.wait_ge(sa_vn, 1)

            def both(i):
                for b in range(2):
                    n = 2 * i + b
                    sample_transposes(n)
                    for half in range(2):
                        sample_scores(i if b == 0 else i + 1, 1 - b, half)
                        lru_gate(i, b, half)
                    for half in range(2):
                        sample_values(n, half)
                    sample_select(n)

            both(0)
            with te.Fori(1, T_XA // 2) as i:
                both(i)
            for n in range(T_XA, NB):
                sample_transposes(n)
                if n + 1 < NB:
                    for half in range(2):
                        sample_scores((n + 1) // 2, (n + 1) % 2, half)
                for half in range(2):
                    sample_values(n, half)
                sample_select(n)

            te.wait_ge(lru_sig, 3 * T_XA)
            te.wait_ge(sa_o, NB)

            def at_round(i):
                def scores(u):
                    h, q, p2, n = u // KD, u % KD, u % 2, P * (u % KD + 1)
                    rows = slice(HD * (h % 2), HD * (h % 2) + HD)
                    te.wait_ge(at_in[h // 2], 48 * (i + 1))
                    wait(te, at_masked, UNITS * i + u - 1)
                    for c in range(0, n, 512):
                        m = min(512, n - c)
                        mm = pe.matmul(ps[:, 2 * p2 + c // 512, 0:m], qkv[rows, h // 2, 0, P * q:P * q + P],
                                       qkv[rows, h // 2, 1, c:c + m], start=True, stop=True)
                    mm.then_inc(at_s, 1)

                def bank_free(g):
                    wait(te, at_pt, GRAN * i + g - 1)

                def values(u):
                    te.wait_ge(at_in[u // 16], 48 * (i + 1))
                    for k, g in enumerate(V_GRAN[u]):
                        bank_free(g)
                        for j in range(4):
                            mm = pe.transpose(ps[:, 4 + g % 2, P * j:P * j + P],
                                              qkv[:, u // 16, 2, P * (4 * k + j):P * (4 * k + j) + P], ident[:])
                        mm.then_inc(at_t, 1)

                def transposes(u):
                    te.wait_ge(at_pn, UNITS * i + u + 1)
                    for k, g in enumerate(P_GRAN[u]):
                        bank_free(g)
                        for j in range(min(4, u % KD + 1 - 4 * k)):
                            mm = pe.transpose(ps[:, 4 + g % 2, P * j:P * j + P],
                                              pm[:, u % 2, P * (4 * k + j):P * (4 * k + j) + P], ident[:])
                        mm.then_inc(at_t, 1)

                def outputs(u):
                    h, q = u // KD, u % KD
                    rows = slice(HD * (h % 2), HD * (h % 2) + HD)
                    te.wait_ge(at_pt, GRAN * i + P_GRAN[u][-1] + 1)
                    if q % 4 == 0:
                        wait(te, at_o, 8 * i + u // 4 - 1)
                    for j in range(q + 1):
                        mm = pe.matmul(ps[rows, 6 + u // 4 % 2, P * (q % 4):P * (q % 4) + P], vn[:, h // 2, j, rows],
                                       pt[:, u % 2, j], start=(j == 0), stop=(j == q))
                    mm.then_inc(at_pv, 1)

                scores(0)
                for x in range(-1, UNITS + 1):
                    if x + 1 < UNITS and (x + 1) % (2 * KD) == 0:
                        values(x + 1)
                    if x + 2 < UNITS:
                        scores(x + 2)
                    if x >= 1:
                        outputs(x - 1)
                    if 0 <= x < UNITS:
                        transposes(x)

            at_round(0)
            with te.Fori(1, HP // 2) as i:
                at_round(i)

            te.wait_ge(at_masked, UNITS * (HP // 2))
            te.wait_ge(at_pt, GRAN * (HP // 2))
            te.wait_ge(at_o, 8 * (HP // 2))

            for m in range(K_B):
                for dst in range(2):
                    product(P_GLU + m // 2, m % 2, range(K_B), dst, K_B * dst, op_hi, op_lo,
                            lambda k: te.wait_ge(op_l, k + 1), USES[P_GLU] + m)
            for m in range(KD // 2):
                for dst in range(2):
                    product(P_B + m // 2, m % 2, range(K_B, 2 * K_B), dst, K_B * dst, op_hi, op_lo,
                            lambda k: te.wait_ge(glu_l, k - K_B + 1), USES[P_B] + m)

            def projection(first, kts, hi, lo, ready):
                u0 = USES[first]
                for b in range(2):
                    product(first, b, kts, b, 0, hi, lo, ready, u0)
                with te.Fori(1, KD // 2) as i:
                    for b in range(2):
                        product(i + first, b, kts, b, 0, hi, lo, nothing, i + u0)

            projection(P_A, range(K_A), hid_hi, hid_lo, lambda k: te.wait_ge(op_l, K_B + k + 1))
            projection(P_C, range(K_C), op_hi, op_lo, lambda k: te.wait_ge(op_l, K_B + K_A + k + 1))
            projection(P_OUT, range(KD), op_hi, op_lo, lambda k: te.wait_ge(o_lo, k + 1))
            sum_squares(n_mix, USES[P_MLP])
            sum_squares(n_pre, 0)

            def up(pair, ready, uses):
                for n in range(FCH):
                    product(pair + n // 2, n % 2, range(KD), n % 2, 0, op_hi, op_lo,
                            ready, uses + n // 2)

            def down(pair, parity, hidden_tiles, uses):
                te.wait_ge(hid_l, hidden_tiles)
                for m in range(KD // 2):
                    for dst in range(2):
                        product(pair + m // 2, m % 2, range(FCH * parity, FCH * parity + FCH), dst, FCH * dst,
                                hid_hi, hid_lo, nothing, uses + m)

            up(P_MLP, lambda k: te.wait_ge(n_pre.lo, k + 1), USES[P_MLP])
            per, u1, p1 = USES[P_MLP + 6] - USES[P_MLP + 2], USES[P_MLP + 2], P_MLP + 2
            with te.Fori(0, (NCH - 2) // 2) as c2:
                for c in range(2):
                    up(c2 * 8 + (4 * c + p1), nothing, c2 * (2 * per) + (c * per + u1))
                    down(c2 * 8 + (4 * c + p1 + 2), c, c2 * (2 * FCH) + FCH * (c + 1), c2 * (2 * per) + (c * per + u1 + 2))
            c = NCH - 2
            up(p1 + 4 * c, nothing, u1 + c * per)
            down(p1 + 4 * c + 2, 0, FCH * (c + 1), u1 + c * per + 2)
            down(p1 + 4 * c + 4, 1, FCH * (c + 2), u1 + (c + 1) * per)
            sum_squares(n_ff, USES[-1])


def _features(a):
    n = a.shape[-1] // P
    return a.reshape(-1, n, P).transpose(2, 1, 0)


def _tiles(w):
    k, m = w.shape
    return w.reshape(k // P, P, m // P, P).transpose(2, 1, 0, 3)


def _doubled(tiles, first, second):
    return np.concatenate([tiles[first], tiles[second]], axis=2)


def _log_count(delta):
    count = sum(((delta >= 0) & (delta <= w) & (delta % d == 0)).astype(np.int64) for w, d in GROUPS)
    return np.where(count > 0, np.log(np.maximum(count, 1)) / SCALE, MASKED).astype(np.float32)


def kernel(**inputs):
    import concourse.bacc as bacc
    from concourse.bass_utils import run_bass_kernel_spmd

    a = {k: np.asarray(x)[0] if k not in ("x_prompt", "x_sample") else np.asarray(x) for k, x in inputs.items()}
    w_in = _tiles(a["w_in"])
    xa, u = slice(0, T_XA), slice(T_XA, T_XA + T_U)
    rest = slice(T_XA + T_U, None)
    glu, pb = _tiles(a["glu_w"]), _tiles(a["w_proj_b"])
    pad = np.zeros((KD, P, KD - K_A, P), np.float32)
    w1, w2 = _tiles(a["mlp_w1"]), [_tiles(a["mlp_w2"][c * FCH * P:(c + 1) * FCH * P]) for c in range(NCH)]
    even, odd = slice(0, None, 2), slice(1, None, 2)
    up = [w1[c * FCH:(c + 1) * FCH] for c in range(NCH)]
    down = [_doubled(w, even, odd) for w in w2]
    mlp = [up[0]]
    for c in range(NCH - 1):
        mlp += [up[c + 1], down[c]]
    mlp.append(down[-1])
    stream = np.concatenate([
        w_in[u], w_in[xa], w_in[rest], _doubled(glu, slice(0, K_B), slice(K_B, None)), _doubled(pb, even, odd),
        np.concatenate([_tiles(a["w_proj_a"]), pad], axis=2), np.concatenate([_tiles(a["w_proj_c"]), pad], axis=2),
        _tiles(a["w_out"])] + mlp)
    blocks = np.zeros((T_XA, P, 2, P), np.float32)
    for n, name in enumerate(("lru_wr", "lru_wi")):
        for h in range(2):
            half = slice(64 * h, 64 * h + 64)
            blocks[:, half, n, half] = a[name][h::2]
    par = np.zeros((T_XA, P, 16), np.float32)
    par[:, :, 0:CW] = a["conv_w"].reshape(CW, T_XA, P).transpose(1, 2, 0)
    par[:, :, 4] = a["conv_b"].reshape(T_XA, P)
    par[:, :, 5] = a["lru_br"].reshape(T_XA, P)
    par[:, :, 6] = a["lru_bi"].reshape(T_XA, P)
    par[:, :, 8:16] = a["state_lru"].reshape(NB, T_XA, P).transpose(1, 2, 0)

    def states(x):
        x = x.reshape((J, 2, NST) + x.shape[2:])
        return np.moveaxis(x, 0, 2).reshape((P, J) + x.shape[3:])

    rows = np.concatenate([np.arange(W_MAX - NEAR, W_MAX),
                           (np.arange(0, W_MAX - NEAR, 16)[:, None] + np.arange(TS)).ravel()])
    kc = a["cache_k"][:, rows].reshape(NB, NCK, HP, P).transpose(0, 3, 2, 1)
    vc = a["cache_v"][:, rows].reshape(NB, KT, P, AW).transpose(0, 2, 1, 3)
    q = np.arange(TS)
    old = _log_count(W_MAX + q[:, None] - rows[None, :])
    sbias = np.tile(old, (HEADS, 1))
    nbias = np.full((HEADS, TS, NB, NB, TS), MASKED, np.float32)
    for b in range(NB):
        nbias[:, :, b, b] = _log_count(q[:, None] - q[None, :])
    omask = np.kron(np.eye(HEADS), np.ones((TS, HD))).astype(np.float32)
    arrays = dict(
        w=stream.reshape(-1, P, KD * P),
        x=np.concatenate([_features(a["x_prompt"]), _features(a["x_sample"])], axis=2),
        ident=np.eye(P, dtype=np.float32), ones=np.ones((P, P), np.float32),
        gains=np.stack([a[k].reshape(KD, P).T for k in ("norm_pre_mix", "norm_post_mix", "norm_pre_mlp", "norm_post_mlp")], 1),
        glu_b=a["glu_b"].reshape(2, K_B, P).transpose(2, 0, 1),
        lam=a["lru_lambda"].reshape(T_XA, P).T,
        lru_w=blocks.reshape(T_XA, P, 2 * P), lru_par=par,
        conv_s=a["state_conv"].reshape(NB, CW - 1, T_XA, P).transpose(2, 3, 0, 1).reshape(T_XA, P, -1),
        s5_par=np.stack([states(a["ssm_lambda_re"]), states(a["ssm_lambda_im"]),
                         states(np.broadcast_to(a["ssm_log_dt"][:, None], (G, NST)))], 1),
        s5_bc=np.stack([np.stack([states(a["ssm_b_re"]), states(a["ssm_b_im"])], 1),
                        np.stack([states(a["ssm_c_re"].transpose(0, 2, 1)), states(a["ssm_c_im"].transpose(0, 2, 1))], 1)], 1),
        s5_d=a["ssm_d"].T,
        s0=np.stack([states(a[k].transpose(1, 2, 0)) for k in ("state_ssm_re", "state_ssm_im")], 1),
        k_cache=kc.reshape(NB, P, -1), v_cache=vc.reshape(NB, P, -1),
        bias=_log_count(T - P + np.arange(P)[:, None] - np.arange(T)[None, :]),
        sbias=sbias, nbias=nbias.reshape(HQ, NB, NS), omask=omask,
        tsel=np.tile(np.eye(TS, dtype=np.float32), (HEADS, 1)),
    )
    outs = dict(y=(P, KD, N), keep=(T_KEEP, P, N), ya=(T_XA, P, N), p_ssm=(P, 2, J), s_ssm=(P, 2, J, NB))
    scratch = dict(u_d=(S5W, N), gate_d=(T_GATE, P, N), y5_d=(S5W, N), yc=(HP, P, N), x2_d=(P, KD, N))
    nc = bacc.Bacc("TRN2", target_bir_lowering=False, num_devices=1)
    feed, t = {}, {}
    for name, x in arrays.items():
        feed["in_" + name] = np.ascontiguousarray(x)
        t[name] = nc.dram_tensor("in_" + name, x.shape, F32, kind="ExternalInput").ap()
    for name, shape in outs.items():
        t[name] = nc.dram_tensor("out_" + name, shape, F32, kind="ExternalOutput").ap()
    for name, shape in scratch.items():
        t[name] = nc.dram_tensor("tmp_" + name, shape, F32, kind="Internal").ap()
    hybrid_layer(nc, t)
    got = run_bass_kernel_spmd(nc, [feed], core_ids=[0]).results[0]
    y, keep, ya, p_ssm, s_ssm = (np.asarray(got["out_" + k]) for k in outs)
    y = y.transpose(2, 1, 0).reshape(N, D)

    def kept(row, tiles, cols):
        return np.moveaxis(keep[row:row + tiles, :, cols], 2, 0).reshape(-1, tiles * P)

    def unstate(x):
        x = x.reshape((2, NST, J) + x.shape[2:])
        x = np.moveaxis(x, 2, 0).reshape((G, NST) + x.shape[3:])
        return np.moveaxis(x, (0, 1), (-2, -1)).reshape((1, -1, G, NST))

    old_new, new = slice(0, T), slice(T, N)
    xs = kept(R_XA, T_XA, new).reshape(NB, TS, LRU)
    return (y[:T].reshape(1, T, D), y[T:].reshape(NB, TS, D),
            kept(R_XA, T_XA, slice(T - CW + 1, T)).reshape(1, 1, CW - 1, LRU),
            ya[:, :, T - 1].reshape(1, 1, LRU),
            unstate(p_ssm[:, 0]), unstate(p_ssm[:, 1]),
            kept(R_K, HP, old_new).reshape(1, 1, T, HEADS, HD), kept(R_V, HP, old_new).reshape(1, 1, T, HEADS, HD),
            xs[:, TS - CW + 1:].reshape(1, NB, CW - 1, LRU),
            ya[:, :, T + TS - 1::TS].transpose(2, 0, 1).reshape(1, NB, LRU),
            unstate(s_ssm[:, 0]), unstate(s_ssm[:, 1]),
            kept(R_K, HP, new).reshape(1, NB, TS, HEADS, HD), kept(R_V, HP, new).reshape(1, NB, TS, HEADS, HD))
```
